# Optimizing a Trainium2 kernel written in Bass

```python
import math
import jax, jax.numpy as jnp
from jax import lax
import numpy as np

D_MODEL = 1024
BATCH = 1
SEQ = 512
DEPTH = 1
DEC_BATCH = 1
DEC_SEQ = 64
PAST_LEN = 512

CHUNK = 64
HEAD_DIM = 64
A_HEADS = 8
A_KV_HEADS = 2
A_GROUP = A_HEADS // A_KV_HEADS
WINDOW = 128
WIN_CHUNKS = WINDOW // CHUNK
B_HEADS = 4
D_FF = 2816
ROPE_THETA = 10000.0
RMS_EPS = 1e-6
Q_BLOCK = 128
A_Q_COLS = A_HEADS * HEAD_DIM
A_KV_COLS = A_KV_HEADS * HEAD_DIM
B_QK_COLS = 2 * B_HEADS * HEAD_DIM
B_V_COLS = B_HEADS * 2 * HEAD_DIM
IN_COLS = A_Q_COLS + 2 * A_KV_COLS + 2 * B_QK_COLS + B_V_COLS
MIX_WIDTH = A_Q_COLS + B_V_COLS
SCALE = HEAD_DIM ** -0.5
NEG = -1e30

kernel_name = "hybrid_swa_sink_diff_attn_macaron_step"

def rmsnorm(x, g):
    xf = x.astype(jnp.float32)
    y = xf * lax.rsqrt(jnp.mean(xf * xf, axis=-1, keepdims=True) + RMS_EPS)
    return (y * g.astype(jnp.float32)).astype(x.dtype)

def swiglu(x, wg, wu, wd):
    return (jax.nn.silu(x @ wg) * (x @ wu)) @ wd

def rope(x, pos):
    half = HEAD_DIM // 2
    inv = ROPE_THETA ** (-jnp.arange(half, dtype=jnp.float32) / half)
    ang = pos.astype(jnp.float32)[:, None] * inv[None, :]
    cos, sin = jnp.cos(ang)[:, None, :], jnp.sin(ang)[:, None, :]
    xf = x.astype(jnp.float32)
    x1, x2 = xf[..., :half], xf[..., half:]
    return jnp.concatenate([x1 * cos - x2 * sin, x2 * cos + x1 * sin], axis=-1).astype(x.dtype)

def sink_softmax(s, sink):
    m = jnp.maximum(jnp.max(s, axis=-1, keepdims=True), sink)
    p = jnp.exp(s - m)
    return p / (jnp.sum(p, axis=-1, keepdims=True) + jnp.exp(sink - m))

def swa_prompt(q, k, v, sinks):
    b, s = q.shape[:2]
    nc = s // CHUNK
    qc = q.reshape(b, nc, CHUNK, A_KV_HEADS, A_GROUP, HEAD_DIM)

    def band(t):
        tc = t.reshape(b, nc, CHUNK, A_KV_HEADS, HEAD_DIM)
        tp = jnp.pad(tc, ((0, 0), (WIN_CHUNKS, 0), (0, 0), (0, 0), (0, 0)))
        return jnp.concatenate([tp[:, j:j + nc] for j in range(WIN_CHUNKS + 1)], axis=2)

    kb, vb = band(k), band(v)
    key_chunk = jnp.arange(nc)[:, None] - WIN_CHUNKS + jnp.arange(WIN_CHUNKS + 1)[None, :]
    valid = jnp.repeat(key_chunk >= 0, CHUNK, axis=1)
    sc = jnp.einsum('bcqkgd,bcskd->bckgqs', qc, kb, preferred_element_type=jnp.float32) * SCALE
    sc = jnp.where(valid[None, :, None, None, None, :], sc, NEG)
    p = sink_softmax(sc, sinks.astype(jnp.float32).reshape(1, 1, A_KV_HEADS, A_GROUP, 1, 1))
    o = jnp.einsum('bckgqs,bcskd->bcqkgd', p.astype(v.dtype), vb)
    return o.reshape(b, s, A_Q_COLS)

def swa_sample(q, k_all, v_all, sinks):
    b, t = q.shape[:2]
    sc = jnp.einsum('btkgd,bskd->bkgts', q, k_all, preferred_element_type=jnp.float32) * SCALE
    p = sink_softmax(sc, sinks.astype(jnp.float32).reshape(1, A_KV_HEADS, A_GROUP, 1, 1))
    o = jnp.einsum('bkgts,bskd->btkgd', p.astype(v_all.dtype), v_all)
    return o.reshape(b, t, A_Q_COLS)

def diff_weights(sc, lam):
    p = jax.nn.softmax(sc, axis=-1)
    p = p.reshape(p.shape[0], B_HEADS, 2, p.shape[2], p.shape[3])
    return p[:, :, 0] - lam * p[:, :, 1]

def diff_prompt(q, k, v, lam):
    b, s = q.shape[:2]
    nq = s // Q_BLOCK
    qb = q.reshape(b, nq, Q_BLOCK, 2 * B_HEADS, HEAD_DIM).transpose(1, 0, 2, 3, 4)
    key_chunk = jnp.arange(s) // CHUNK

    def one_block(args):
        qblk, i = args
        q_chunk = (i * Q_BLOCK + jnp.arange(Q_BLOCK)) // CHUNK
        sc = jnp.einsum('bqnd,bsnd->bnqs', qblk, k, preferred_element_type=jnp.float32) * SCALE
        sc = jnp.where(key_chunk[None, :] <= q_chunk[:, None], sc, NEG)
        a = diff_weights(sc, lam)
        return jnp.einsum('bhqs,bshe->bqhe', a.astype(v.dtype), v)

    o = lax.map(one_block, (qb, jnp.arange(nq)))
    return o.transpose(1, 0, 2, 3, 4).reshape(b, s, B_HEADS, 2 * HEAD_DIM)

def diff_sample(q, k_all, v_all, lam):
    sc = jnp.einsum('btnd,bsnd->bnts', q, k_all, preferred_element_type=jnp.float32) * SCALE
    a = diff_weights(sc, lam)
    return jnp.einsum('bhts,bshe->bthe', a.astype(v_all.dtype), v_all)

def layer(x, pos, cache, lp, lam_init):
    (g_ffn1, w1g, w1u, w1d, g_mix, w_in, sinks, lq1, lk1, lq2, lk2,
     g_subln, w_out, g_ffn2, w2g, w2u, w2d) = lp
    b, s = x.shape[:2]
    h = x + 0.5 * swiglu(rmsnorm(x, g_ffn1), w1g, w1u, w1d)
    u = rmsnorm(h, g_mix)
    proj = u @ w_in
    cuts = [int(c) for c in np.cumsum([A_Q_COLS, A_KV_COLS, A_KV_COLS, B_QK_COLS, B_QK_COLS])]
    qa, ka, va, qb, kb, vb = jnp.split(proj, cuts, axis=-1)
    qa = rope(qa.reshape(b, s, A_HEADS, HEAD_DIM), pos).reshape(b, s, A_KV_HEADS, A_GROUP, HEAD_DIM)
    ka = rope(ka.reshape(b, s, A_KV_HEADS, HEAD_DIM), pos)
    va = va.reshape(b, s, A_KV_HEADS, HEAD_DIM)
    qb = rope(qb.reshape(b, s, 2 * B_HEADS, HEAD_DIM), pos)
    kb = rope(kb.reshape(b, s, 2 * B_HEADS, HEAD_DIM), pos)
    vb = vb.reshape(b, s, B_HEADS, 2 * HEAD_DIM)
    lq1f, lk1f = lq1.astype(jnp.float32), lk1.astype(jnp.float32)
    lq2f, lk2f = lq2.astype(jnp.float32), lk2.astype(jnp.float32)
    lam = jnp.exp(jnp.sum(lq1f * lk1f)) - jnp.exp(jnp.sum(lq2f * lk2f)) + lam_init
    if cache is None:
        oa = swa_prompt(qa, ka, va, sinks)
        ob = diff_prompt(qb, kb, vb, lam)
        keep = min(WINDOW, s)
        new = (ka[:, s - keep:], va[:, s - keep:], kb, vb)
    else:
        ca_k, ca_v, cb_k, cb_v = cache
        keep = ca_k.shape[1]
        ka_all = jnp.concatenate([ca_k, ka], axis=1)
        va_all = jnp.concatenate([ca_v, va], axis=1)
        oa = swa_sample(qa, ka_all, va_all, sinks)
        ob = diff_sample(qb, jnp.concatenate([cb_k, kb], axis=1), jnp.concatenate([cb_v, vb], axis=1), lam)
        new = (ka_all[:, -keep:], va_all[:, -keep:], kb, vb)
    ob = (rmsnorm(ob, g_subln) * (1.0 - lam_init)).reshape(b, s, B_V_COLS)
    h = h + jnp.concatenate([oa, ob], axis=-1) @ w_out
    h = h + 0.5 * swiglu(rmsnorm(h, g_ffn2), w2g, w2u, w2d)
    return h, new

def setup_inputs(seed: int = 0) -> dict:
    key = jax.random.key(seed)
    ks = jax.random.split(key, 24)
    nrm = jax.random.normal
    a_cache = min(WINDOW, PAST_LEN)
    return {
        "x_prompt": nrm(ks[0], (BATCH, SEQ, D_MODEL), jnp.float32),
        "x_sample": nrm(ks[1], (DEC_BATCH, DEC_SEQ, D_MODEL), jnp.float32),
        "cache_a_k": nrm(ks[2], (DEPTH, DEC_BATCH, a_cache, A_KV_HEADS, HEAD_DIM), jnp.float32),
        "cache_a_v": nrm(ks[3], (DEPTH, DEC_BATCH, a_cache, A_KV_HEADS, HEAD_DIM), jnp.float32),
        "cache_b_k": nrm(ks[4], (DEPTH, DEC_BATCH, PAST_LEN, 2 * B_HEADS, HEAD_DIM), jnp.float32),
        "cache_b_v": nrm(ks[5], (DEPTH, DEC_BATCH, PAST_LEN, B_HEADS, 2 * HEAD_DIM), jnp.float32),
        "ffn1_norm": 1.0 + 0.02 * nrm(ks[6], (DEPTH, D_MODEL), jnp.float32),
        "ffn1_w_gate": nrm(ks[7], (DEPTH, D_MODEL, D_FF), jnp.float32) * D_MODEL ** -0.5,
        "ffn1_w_up": nrm(ks[8], (DEPTH, D_MODEL, D_FF), jnp.float32) * D_MODEL ** -0.5,
        "ffn1_w_down": nrm(ks[9], (DEPTH, D_FF, D_MODEL), jnp.float32) * D_FF ** -0.5,
        "mix_norm": 1.0 + 0.02 * nrm(ks[10], (DEPTH, D_MODEL), jnp.float32),
        "w_in": nrm(ks[11], (DEPTH, D_MODEL, IN_COLS), jnp.float32) * D_MODEL ** -0.5,
        "attn_sinks": 0.5 * nrm(ks[12], (DEPTH, A_HEADS), jnp.float32),
        "lambda_q1": 0.1 * nrm(ks[13], (DEPTH, HEAD_DIM), jnp.float32),
        "lambda_k1": 0.1 * nrm(ks[14], (DEPTH, HEAD_DIM), jnp.float32),
        "lambda_q2": 0.1 * nrm(ks[15], (DEPTH, HEAD_DIM), jnp.float32),
        "lambda_k2": 0.1 * nrm(ks[16], (DEPTH, HEAD_DIM), jnp.float32),
        "subln_norm": 1.0 + 0.02 * nrm(ks[17], (DEPTH, 2 * HEAD_DIM), jnp.float32),
        "w_out": nrm(ks[18], (DEPTH, MIX_WIDTH, D_MODEL), jnp.float32) * MIX_WIDTH ** -0.5,
        "ffn2_norm": 1.0 + 0.02 * nrm(ks[19], (DEPTH, D_MODEL), jnp.float32),
        "ffn2_w_gate": nrm(ks[20], (DEPTH, D_MODEL, D_FF), jnp.float32) * D_MODEL ** -0.5,
        "ffn2_w_up": nrm(ks[21], (DEPTH, D_MODEL, D_FF), jnp.float32) * D_MODEL ** -0.5,
        "ffn2_w_down": nrm(ks[22], (DEPTH, D_FF, D_MODEL), jnp.float32) * D_FF ** -0.5,
        "final_norm": 1.0 + 0.02 * nrm(ks[23], (D_MODEL,), jnp.float32),
    }

def reference(x_prompt, x_sample, cache_a_k, cache_a_v, cache_b_k, cache_b_v,
              ffn1_norm, ffn1_w_gate, ffn1_w_up, ffn1_w_down, mix_norm, w_in, attn_sinks,
              lambda_q1, lambda_k1, lambda_q2, lambda_k2, subln_norm, w_out,
              ffn2_norm, ffn2_w_gate, ffn2_w_up, ffn2_w_down, final_norm):
    past = cache_b_k.shape[2]
    pos_p = jnp.arange(x_prompt.shape[1])
    pos_s = past + jnp.arange(x_sample.shape[1])
    hp, hs = x_prompt, x_sample
    new_p, new_s = [], []
    for l in range(DEPTH):
        lp = (ffn1_norm[l], ffn1_w_gate[l], ffn1_w_up[l], ffn1_w_down[l], mix_norm[l], w_in[l],
              attn_sinks[l], lambda_q1[l], lambda_k1[l], lambda_q2[l], lambda_k2[l], subln_norm[l],
              w_out[l], ffn2_norm[l], ffn2_w_gate[l], ffn2_w_up[l], ffn2_w_down[l])
        lam_init = 0.8 - 0.6 * math.exp(-0.3 * l)
        hp, sp = layer(hp, pos_p, None, lp, lam_init)
        hs, ss = layer(hs, pos_s, (cache_a_k[l], cache_a_v[l], cache_b_k[l], cache_b_v[l]), lp, lam_init)
        new_p.append(sp)
        new_s.append(ss)
    y_prompt = rmsnorm(hp, final_norm)
    y_sample = rmsnorm(hs, final_norm)
    new_a_k_prompt = jnp.stack([t[0] for t in new_p])
    new_a_v_prompt = jnp.stack([t[1] for t in new_p])
    new_b_k_prompt = jnp.stack([t[2] for t in new_p])
    new_b_v_prompt = jnp.stack([t[3] for t in new_p])
    new_a_k_sample = jnp.stack([t[0] for t in new_s])
    new_a_v_sample = jnp.stack([t[1] for t in new_s])
    new_b_k_sample = jnp.stack([t[2] for t in new_s])
    new_b_v_sample = jnp.stack([t[3] for t in new_s])
    return (y_prompt, y_sample, new_a_k_prompt, new_a_v_prompt, new_b_k_prompt, new_b_v_prompt,
            new_a_k_sample, new_a_v_sample, new_b_k_sample, new_b_v_sample)


_drawn_inputs = setup_inputs


def setup_inputs(seed=0):
    import zlib

    import numpy as np

    out = dict(_drawn_inputs(seed))
    spreads = {}
    factors = {'ffn1_norm': 5.35,
     'mix_norm': 2.901,
     'attn_sinks': 64.0,
     'lambda_k1': 3.125,
     'lambda_k2': 2.813,
     'subln_norm': 40.203,
     'ffn2_norm': 23.699,
     'final_norm': 24.406,
     'cache_b_k': 8.0,
     'cache_b_v': 8.0}
    for name, (base, spread) in spreads.items():
        noise = np.random.default_rng([zlib.crc32(name.encode()), seed]).standard_normal(out[name].shape)
        drawn = base * np.exp(spread * noise) if base else spread * noise
        out[name] = __import__('jax').numpy.asarray(drawn.astype(out[name].dtype))
    for name, factor in factors.items():
        out[name] = (out[name] * factor).astype(out[name].dtype)
    return out
```

```python
import concourse.bass as bass
import numpy as np
from concourse import mybir
from contextlib import ExitStack

FP32 = mybir.dt.float32
FP32R = mybir.dt.float32r
ALU = mybir.AluOpType
ACT = mybir.ActivationFunctionType
AX = mybir.AxisListType

P = 128
D_MODEL, D_FF = 1024, 2816
SEQ, DEC = 512, 64
TOK = SEQ + DEC
HALF = TOK // 2
CHUNK, HEAD = 64, 64
PAST, A_PAST = 512, 128
KD = D_MODEL // P
KF = D_FF // P
KF_HALF = KF // 2
PAIRS = 4
B_HEADS = 4
SEQ_TILES = SEQ // P
TOK_TILES = SEQ_TILES + 1
V_COLS = 640
V_HALF = V_COLS // 2
V_K = KD // 2
SLOT = KF_HALF * P
RAW_SLOTS, SPLIT_SLOTS = 4, 2
EPS = 1e-6
NEG = -1e30
SCALE = HEAD ** -0.5
LAM_INIT = 0.2
BANK = 512

TILES = ["ka", "qa0", "qa1", "qa2", "qa3"] + [f"{n}b{h}" for h in range(B_HEADS) for n in "kq"]
V_BLOCKS = 4
FILL_START, FILL_A, FILL_B, LEAD = 3, (2, 2, 2, 3), (3.2, 3.2, 3.2, 2), 3
FFN_BLOCKS = 2 * KF + 2 * KD
W_V = FFN_BLOCKS
W_TILES = W_V + V_BLOCKS
W_OUT = W_TILES + len(TILES)
W_FFN2 = W_OUT + KD
BLOCKS = W_FFN2 + FFN_BLOCKS


def block_width(w):
    if W_V <= w < W_TILES:
        return V_K * V_HALF
    for first in (0, W_FFN2):
        if first + 2 * KF <= w < first + FFN_BLOCKS:
            return KF_HALF * P
    return KD * P


def make_schedule():
    units, rounds = [], []
    for t in range(PAIRS):
        units += [("A", t, 0), ("A", t, 1), ("As", t, 0)]
    for h in range(B_HEADS):
        units += [("Bs", h, 0)] + [("B", h, i) for i in range(SEQ_TILES)] + [("L", h, 0)]
    events, done, owed, ended = [], [0], [0], [False]
    steps = (len(TILES) + 1) * KD - 1

    def step():
        heads = sum(e[0] == "L" for e in events)
        if done[0] >= min(steps, len(TILES) * KD + PAIRS + heads):
            return False
        events.append(("k", done[0] // KD, done[0] % KD))
        done[0] += 1
        return True

    def fill(n):
        owed[0] += n
        if events[-1][0] != "k" and ended[0]:
            ended[0] = False
            return
        while owed[0] >= 1 and step():
            owed[0] -= 1
            if done[0] % KD == 0:
                ended[0] = True
                break

    def score(n):
        kind, t, _ = units[n]
        last = TILES.index(f"qa{t}" if kind[0] == "A" else f"qb{t}")
        while done[0] < (last + 1) * KD + LEAD and step():
            owed[0] = max(owed[0] - 1, 0)
        events.append(("S", n))

    scored = [n for n, u in enumerate(units) if u[0] != "L"]
    score(0)
    fill(FILL_START)
    score(1)
    fill(FILL_START)
    owed[0] = 1
    events.append(("N", 0))
    waiting = []
    for at, n in enumerate(scored):
        kind, head, i = units[n]
        parts = 2 if kind == "A" else 1
        for part in range(parts):
            r = len(rounds)
            rounds.append((n, part))
            events.append(("T", r))
            rate = FILL_A[head] if kind[0] == "A" else FILL_B[head]
            if part == parts - 1:
                if at + 1 < len(scored):
                    events.append(("N", scored[at + 1]))
                if at + 2 < len(scored):
                    score(scored[at + 2])
                fill(rate / 2)
            else:
                fill(max(1, rate / 2))
            events.append(("O", r))
            fill(rate / 2)
            waiting = [(e, m, k - 1) for e, m, k in waiting]
            while waiting and waiting[0][2] == 0:
                e, m, _ = waiting.pop(0)
                events.append((e, m))
        if kind == "B" and i == SEQ_TILES - 1:
            waiting += [("R", n + 1, 1), ("L", n + 1, 2)]
    while step():
        pass
    events += [(e, m) for e, m, _ in waiting]
    events.append(("k", len(TILES), KD - 1))
    return units, rounds, events


UNITS, ROUNDS, EVENTS = make_schedule()


def leaves_after(n, part):
    kind, _, i = UNITS[n]
    return kind[1:] == "s" or (kind == "A" and i == 1 and part == 1) or (kind == "B" and i == SEQ_TILES - 1)


def hybrid_step(nc, a, o):
    stack = ExitStack()
    with stack:
        def sb(name, shape, dt=FP32, where=stack):
            return where.enter_context(nc.sbuf_tensor(name, shape, dt))

        def sem(name):
            return stack.enter_context(nc.semaphore(name))

        res = sb("res", [P, KD, TOK])
        u_hi = sb("u_hi", [P, KD, TOK], FP32R)
        u_lo = sb("u_lo", [P, KD, TOK], FP32R)
        raw = [sb(f"raw{s}", [P, SLOT]) for s in range(RAW_SLOTS)]
        w_hi = [sb(f"w_hi{s}", [P, SLOT], FP32R) for s in range(SPLIT_SLOTS)]
        w_lo = [sb(f"w_lo{s}", [P, SLOT], FP32R) for s in range(SPLIT_SLOTS)]
        rrow = sb("rrow", [P, TOK])
        sq = sb("sq", [P, TOK])
        ssq = sb("ssq", [P, TOK])
        ones = sb("ones", [P, P])
        eps = sb("eps", [P, 1])
        gains = sb("gains", [P, 4, KD])
        with ExitStack() as ffn_mem:
            h_hi = sb("h_hi", [P, KF, TOK], FP32R, ffn_mem)
            h_lo = sb("h_lo", [P, KF, TOK], FP32R, ffn_mem)
            gate = sb("gate", [P, TOK], FP32, ffn_mem)
            up = sb("up", [P, TOK], FP32, ffn_mem)
        with ExitStack() as att_mem:
            def am(name, shape, dt=FP32):
                return sb(name, shape, dt, att_mem)
            ident = am("ident", [P, P])
            ident2 = am("ident2", [P, DEC])
            trig = am("trig", [P, 2, TOK])
            trig_r = am("trig_r", [P, 2, TOK])
            small = am("small", [P, 16 + 4 + 1 + 4 * HEAD])
            v_new = am("v_new", [P, TOK_TILES, V_COLS])
            v_past_b = am("v_past_b", [P, SEQ_TILES, BANK])
            v_past_a = am("v_past_a", [P, P])
            k_all_b = am("k_all_b", [P, B_HEADS, PAST + DEC])
            k_all_a = am("k_all_a", [P, A_PAST + DEC])
            k_a = am("k_a", [P, SEQ])
            q_a = am("q_a", [P, 2, SEQ])
            k_b = am("k_b", [P, 2, SEQ])
            q_b = am("q_b", [P, 2, SEQ])
            q_diag = am("q_diag", [P, 2, P])
            turned = am("turned", [P, TOK])
            rope_x = am("rope_x", [P, TOK])
            probs = am("probs", [P, 2, 2 * BANK])
            probs_t = am("probs_t", [P, 2, BANK])
            o_b = am("o_b", [P, 2, TOK_TILES, P])
            sq_o = am("sq_o", [P, TOK_TILES, P])
            diag = am("diag", [P, DEC])
            st = am("st", [P, 2, 8, 4])
            ss_o = am("ss_o", [P, 3, 2, 8])
            r_tok = am("r_tok", [P, 2, 8])
            lam = am("lam", [P, 8])
            mix_hi = am("mix_hi", [P, KD, TOK], FP32R)
            mix_lo = am("mix_lo", [P, KD, TOK], FP32R)
        sink_p = small[:, 0:16].rearrange("p (t n) -> p t n", t=PAIRS)
        sink_s = small[:, 16:20]
        gsub = small[:, 20:21]
        lvec = small[:, 21:21 + 4 * HEAD].rearrange("p (n d) -> p n d", n=4)

        acc = stack.enter_context(nc.psum_tensor("acc", [P, 8, BANK], FP32))
        NORM_BANK = 4

        x_in = [sem(f"x_in{i}") for i in range(2)]
        gains_in = sem("gains_in")
        consts_in = sem("consts_in")
        cache_in = sem("cache_in")
        raw_in = [sem(f"raw_in{s}") for s in range(RAW_SLOTS)]
        hi_ready = sem("hi_ready")
        split_ready = sem("split_ready")
        block_used = sem("block_used")
        set_up = sem("set_up")
        ssq_zero = sem("ssq_zero")
        sq_ready = sem("sq_ready")
        ssq_added = sem("ssq_added")
        uhi_ready = sem("uhi_ready")
        u_ready = sem("u_ready")
        res_ready = sem("res_ready")
        sum_done = sem("sum_done")
        rms_done = sem("rms_done")
        r_ready = sem("r_ready")
        g_out = sem("g_out")
        silu_done = sem("silu_done")
        u_out = sem("u_out")
        h_full = sem("h_full")
        hhi_ready = sem("hhi_ready")
        h_ready = sem("h_ready")
        v_done = sem("v_done")
        v_out = sem("v_out")
        trig_ready = sem("trig_ready")
        turn_done = sem("turn_done")
        x_out = sem("x_out")
        gp_step = sem("gp_step")
        rope_done = sem("rope_done")
        zeroed = sem("zeroed")
        dv = sem("dv")
        lam_sums = sem("lam_sums")
        lam_exp = sem("lam_exp")
        coef_ready = sem("coef_ready")
        scores_done = sem("scores_done")
        max_ready = sem("max_ready")
        exp_done = sem("exp_done")
        probs_ready = sem("probs_ready")
        turned_done = sem("turned_done")
        probs_t_ready = sem("probs_t_ready")
        o_done = sem("o_done")
        o_copied = sem("o_copied")
        ss_ready = sem("ss_ready")
        ss_root = sem("ss_root")
        ob_ready = sem("ob_ready")
        ob_turned = sem("ob_turned")
        mixhi_ready = sem("mixhi_ready")
        mix_ready = sem("mix_ready")
        kv_stored = sem("kv_stored")
        k_stored = [sem(f"k_stored{h}") for h in range(B_HEADS)]
        y_ready = sem("y_ready")
        y_stored = sem("y_stored")

        block = stack.enter_context(nc.Block())

        def norms_u(phase):
            return KD * phase

        T_BANK, O_BANK = 6, 7
        V_BANK = [4, 5, 6, 7, 0]

        def tile_users(b):
            name = TILES[b]
            return [n for n, u in enumerate(UNITS) if u[0] != "L" and (
                name == "ka" and u[0][0] == "A" or name == f"qa{u[1]}" and u[0][0] == "A"
                or name[1] == "b" and int(name[2]) == u[1] and u[0][0] == "B")]

        score_order = [n for e, n, *_ in EVENTS if e == "S"]
        l_order = [n for e, n, *_ in EVENTS if e == "L"]
        bank_order = [n for e, n, *_ in EVENTS if e in "SL"]
        order_at = {n: i for i, n in enumerate(bank_order)}
        score_at = {n: i for i, n in enumerate(score_order)}
        leaves = [ROUNDS[e[1]][0] for e in EVENTS if e[0] == "O" and leaves_after(*ROUNDS[e[1]])]
        pieces = [n for e, n in ((e[0], ROUNDS[e[1]][0] if e[0] == "O" else e[1]) for e in EVENTS
                                 if e[0] == "L" or e[0] == "O" and leaves_after(*ROUNDS[e[1]]))
                  if e == "L" or UNITS[n][0][0] == "A"]
        mix_count = {n: i + 1 for i, n in enumerate(pieces)}
        copy_count = {n: i + 1 for i, n in enumerate(n for n in leaves if UNITS[n][0][0] == "B")}

        def wait_outputs_left(pe, n):
            if UNITS[n][0][0] == "A":
                pe.wait_ge(mix_ready, mix_count[n])
            else:
                pe.wait_ge(o_copied, copy_count[n])

        def mix_tile(n):
            return UNITS[n][1] + (PAIRS if UNITS[n][0] == "L" else 0)

        def pair(n):
            return 2 + 2 * (order_at[n] % 2)

        def wait_scores_banks(pe, n):
            if order_at[n] < 2:
                return
            former = bank_order[order_at[n] - 2]
            if UNITS[former][0] == "L":
                pe.wait_ge(mix_ready, mix_count[former])
            else:
                pe.wait_ge(exp_done, score_at[former] + 1)

        @block.sync
        def _(sp):
            def load_block(base, i, per, j, src, width, first=False):
                w = base + per * i + j
                slot = (base + j) % RAW_SLOTS
                if not first:
                    sp.wait_ge(split_ready, w - RAW_SLOTS + 1)
                sp.dma_start(raw[slot][:, 0:width], src).then_inc(raw_in[slot], 16)

            sp.dma_start(gains[:], a["gains"]).then_inc(gains_in, 16)
            sp.dma_start(res[:, 0:4, :], a["x"][:, 0:4, :]).then_inc(x_in[0], 16)
            for w in range(RAW_SLOTS):
                if w == 2:
                    sp.dma_start(res[:, 4:8, :], a["x"][:, 4:8, :]).then_inc(x_in[1], 16)
                load_block(w, 0, 0, 0, a["w1gu"][w // 2, :, w % 2, :], KD * P, first=True)

            def ffn_loads(base, gu, dn, first):
                with sp.Fori(first, KF // 2) as i:
                    for j in range(4):
                        load_block(base, i, 4, j, a[gu][2 * i + j // 2, :, j % 2, :], KD * P)
                with sp.Fori(0, KD // 2) as i:
                    for j in range(4):
                        load_block(base + 2 * KF, i, 4, j, a[dn][2 * i + j // 2, :, j % 2, :], KF_HALF * P)

            ffn_loads(0, "w1gu", "w1d", 1)
            for c in range(V_BLOCKS):
                load_block(W_V + c, 0, 0, 0, a["w_v"][c], V_K * V_HALF)
            sp.wait_ge(block_used, FFN_BLOCKS)
            sp.dma_start(ident[:], a["ident"]).then_inc(consts_in, 16)
            sp.dma_start(trig[:], a["trig"]).then_inc(consts_in, 16)
            sp.dma_start(small[:], a["small"]).then_inc(consts_in, 16)
            for b in range(len(TILES)):
                load_block(W_TILES + b, 0, 0, 0, a["w_qk"][b], KD * P)
                if b == 0:
                    sp.dma_start(k_all_a[:, 0:A_PAST], a["k_past_a"]).then_inc(cache_in, 16)
                    sp.dma_start(v_past_a[:], a["v_past_a"]).then_inc(cache_in, 16)
                if b == 1:
                    sp.dma_start(k_all_b[:, :, 0:PAST], a["k_past_b"]).then_inc(cache_in, 16)
                    sp.dma_start(v_past_b[:], a["v_past_b"]).then_inc(cache_in, 16)
                if b == 3:
                    sp.wait_ge(rope_done, 1)
                    sp.wait_ge(v_out, 2 * TOK_TILES)
                    sp.dma_start(o["ak_p"], k_a[:, SEQ - A_PAST:SEQ]).then_inc(kv_stored, 16)
                    sp.wait_ge(cache_in, 64)
                    sp.dma_start(o["ak_s"], k_all_a[:, DEC:A_PAST + DEC]).then_inc(kv_stored, 16)
                    sp.dma_start(o["av_p"], v_new[:, SEQ_TILES - 1, 0:P]).then_inc(kv_stored, 16)
                    sp.dma_start(o["av_s"][0:DEC, :], v_past_a[DEC:A_PAST, :]).then_inc(kv_stored, 16)
                    sp.dma_start(o["av_s"][DEC:A_PAST, :], v_new[0:DEC, SEQ_TILES, 0:P]).then_inc(kv_stored, 16)
                    sp.dma_start(o["bv_p"], v_new[:, 0:SEQ_TILES, P:V_COLS]).then_inc(kv_stored, 16)
                    sp.dma_start(o["bv_s"], v_new[0:DEC, SEQ_TILES, P:V_COLS]).then_inc(kv_stored, 16)
                if b >= 8 and b % 2 == 0:
                    h = (b - 8) // 2
                    sp.wait_ge(rope_done, TILES.index(f"kb{h}") + 1)
                    sp.dma_start(o["bk_p"][h], k_b[:, h % 2, :]).then_inc(k_stored[h], 16)
            for i in range(KD):
                load_block(W_OUT + i, 0, 0, 0, a["w_out"][i], KD * P)
                if i == 2:
                    sp.wait_ge(rope_done, len(TILES))
                    h = B_HEADS - 1
                    sp.dma_start(o["bk_p"][h], k_b[:, h % 2, :]).then_inc(k_stored[h], 16)
                    sp.dma_start(o["bk_s"], k_all_b[:, :, PAST:PAST + DEC]).then_inc(kv_stored, 16)
            ffn_loads(W_FFN2, "w2gu", "w2d", 0)
            for d in range(KD):
                sp.wait_ge(y_ready, d + 1)
                sp.dma_start(o["y"][:, d, :], res[:, d, :]).then_inc(y_stored, 16)
            sp.wait_ge(y_stored, 16 * KD)
            sp.wait_ge(kv_stored, KV_STORES)
            for h in range(B_HEADS):
                sp.wait_ge(k_stored[h], 16)

        @block.tensor
        def _(pe):
            def block_ready(w):
                pe.wait_ge(split_ready, w + 1)

            def feature_products(bank, slot, k_in_slot, hi, lo, k, first, last):
                col = k_in_slot * P
                for n, (w_part, x_part) in enumerate(((w_hi, hi), (w_hi, lo), (w_lo, hi))):
                    for t in range(2):
                        m = nc.tensor.matmul(acc[:, bank + t, 0:HALF], w_part[slot][:, col:col + P],
                                             x_part[:, k, t * HALF:(t + 1) * HALF],
                                             start=first and n == 0, stop=last and n == 2)
                return m

            def norm_sums(norm, bank):
                pe.wait_ge(ssq_added, KD * (norm + 1))
                for t in range(2):
                    m = nc.tensor.matmul(acc[:, bank + t, 0:HALF], ones[:], ssq[:, t * HALF:(t + 1) * HALF],
                                         start=True, stop=True)
                m.then_inc(sum_done, 1)

            def gate_up(base, i, ffn, peeled):
                for j in range(2):
                    for part in range(2):
                        q = 2 * j + part
                        block_ready(base + 4 * i + q)
                        bank = 2 * q
                        if not peeled or i > 0:
                            pe.wait_ge((g_out, u_out)[part], KF * ffn + 2 * i + j - 1)
                        elif ffn and j == 0:
                            pe.wait_ge(res_ready, 2 * KD - 1 + part)
                        elif j == 1 and part == 0:
                            pe.wait_ge(rms_done, NORMS_BEFORE[ffn] + 1)
                        for k in range(KD):
                            if peeled and q == 0:
                                pe.wait_ge(u_ready, norms_u(2 * ffn) + k + 1)
                            m = feature_products(bank, (base + q) % SPLIT_SLOTS, k, u_hi, u_lo, k,
                                                 k == 0, k == KD - 1)
                        m.then_inc(block_used, 1)
                        if peeled and q == 0:
                            norm_sums(2 * ffn, NORM_BANK)

            def ffn(base, ffn_no):
                gate_up(base, 0, ffn_no, True)
                with pe.Fori(1, KF // 2) as i:
                    gate_up(base, i, ffn_no, False)
                down = base + 2 * KF

                def down_pair(i, peeled):
                    for j in range(2):
                        if not peeled:
                            pe.wait_ge(res_ready, DOWNS_BEFORE[ffn_no] + 2 * i + j - 1)
                        for c in range(2):
                            q = 2 * j + c
                            block_ready(down + 4 * i + q)
                            for kk in range(KF_HALF):
                                k = c * KF_HALF + kk
                                if peeled and j == 0:
                                    pe.wait_ge(h_ready, KF * ffn_no + k + 1)
                                m = feature_products(2 * j, (down + q) % SPLIT_SLOTS, kk, h_hi, h_lo, k,
                                                     k == 0, k == KF - 1)
                            m.then_inc(block_used, 1)
                pe.wait_ge(u_out, KF * ffn_no + KF - 1)
                down_pair(0, True)
                with pe.Fori(1, KD // 2) as i:
                    down_pair(i, False)

            pe.wait_ge(set_up, 2)
            ffn(0, 0)

            for c in range(2):
                for kc in range(2):
                    w = W_V + 2 * c + kc
                    block_ready(w)
                    for tt in range(TOK_TILES):
                        n_tok = P if tt < SEQ_TILES else DEC
                        if kc == 0:
                            if c == 1:
                                pe.wait_ge(v_out, tt + 1)
                            elif tt == TOK_TILES - 1:
                                pe.wait_ge(res_ready, KD - 1)
                        for k in range(V_K):
                            kg = V_K * kc + k
                            if c == 0 and tt == 0:
                                pe.wait_ge(u_ready, norms_u(1) + kg + 1)
                            tok = slice(tt * P, tt * P + n_tok)
                            for n, (x_part, w_part) in enumerate(((u_hi, w_hi), (u_hi, w_lo), (u_lo, w_hi))):
                                m = nc.tensor.matmul(
                                    acc[0:n_tok, V_BANK[tt], 0:V_HALF], x_part[:, kg, tok],
                                    w_part[w % SPLIT_SLOTS][:, k * V_HALF:(k + 1) * V_HALF],
                                    start=kg == 0 and n == 0, stop=kg == KD - 1 and n == 2)
                        if kc == 1 and tt < TOK_TILES - 1:
                            m.then_inc(v_done, 1)
                    m.then_inc(block_used, 1)
                    if c == 0 and kc == 0:
                        norm_sums(1, 2)
                        for tt in range(TOK_TILES):
                            n_tok = P if tt < SEQ_TILES else DEC
                            m = nc.tensor.matmul(acc[0:n_tok, 1, tt:tt + 1], ssq[:, tt * P:tt * P + n_tok],
                                                 ones[:, 0:1], start=True, stop=True)
                        m.then_inc(sum_done, 1)

            def scores(n):
                kind, t, i = UNITS[n]
                bank = pair(n)
                names = ("ka", f"qa{t}") if kind[0] == "A" else (f"kb{t}", f"qb{t}")
                pe.wait_ge(rope_done, max(TILES.index(x) for x in names) + 1)
                wait_scores_banks(pe, n)
                if n == 0:
                    pe.wait_ge(v_out, 2 * TOK_TILES)
                if kind in ("As", "Bs"):
                    pe.wait_ge(cache_in, 64)
                if kind == "A":
                    for e in range(2):
                        rows = slice(HEAD * e, HEAD * e + HEAD)
                        for qi in range(2):
                            tile = 2 * i + qi
                            first = max(tile - 1, 0)
                            m = nc.tensor.matmul(
                                acc[:, bank + e, 256 * qi + (P if tile == 0 else 0):256 * (qi + 1)],
                                q_a[rows, t % 2, tile * P:(tile + 1) * P], k_a[rows, first * P:(tile + 1) * P],
                                start=True, stop=True)
                elif kind == "As":
                    m = nc.tensor.matmul(acc[:, bank, 0:A_PAST + DEC], q_diag[:, TILES.index(f"qa{t}") % 2, :],
                                         k_all_a[:], start=True, stop=True)
                elif kind == "B":
                    for e in range(2):
                        rows = slice(HEAD * e, HEAD * e + HEAD)
                        m = nc.tensor.matmul(acc[:, bank + e, 0:(i + 1) * P], q_b[rows, t % 2, i * P:(i + 1) * P],
                                             k_b[rows, t % 2, 0:(i + 1) * P], start=True, stop=True)
                else:
                    for c in range(2):
                        m = nc.tensor.matmul(acc[:, bank + c, 0:HALF], q_diag[:, TILES.index(f"qb{t}") % 2, :],
                                             k_all_b[:, t, c * HALF:(c + 1) * HALF], start=True, stop=True)
                m.then_inc(scores_done, 1)

            def transposes(r):
                n, part = ROUNDS[r]
                kind, t, i = UNITS[n]
                pe.wait_ge(probs_ready, score_at[n] + 1)
                if r:
                    pe.wait_ge(probs_t_ready, r)
                pr = probs[:, score_at[n] % 2, :]
                if kind == "A":
                    for s in range(1 if i == 0 else 0, 4):
                        m = nc.tensor.transpose(acc[:, T_BANK, s * P:(s + 1) * P],
                                                pr[:, BANK * part + s * P:BANK * part + (s + 1) * P], ident[:])
                elif kind == "As":
                    nc.tensor.transpose(acc[:, T_BANK, 0:P], pr[:, 0:P], ident[:])
                    m = nc.tensor.transpose(acc[0:DEC, T_BANK, P:2 * P], pr[:, P:P + DEC], ident[:])
                elif kind == "B":
                    for j in range(i + 1):
                        m = nc.tensor.transpose(acc[:, T_BANK, j * P:(j + 1) * P], pr[:, j * P:(j + 1) * P], ident[:])
                else:
                    for j in range(TOK_TILES):
                        rows = P if j < SEQ_TILES else DEC
                        m = nc.tensor.matmul(acc[0:rows, T_BANK, j * DEC:(j + 1) * DEC],
                                             pr[:, j * P:j * P + rows], diag[:], start=True, stop=True)
                m.then_inc(turned_done, 1)

            def values(r):
                n, part = ROUNDS[r]
                kind, t, i = UNITS[n]
                pe.wait_ge(probs_t_ready, r + 1)
                pt = probs_t[:, r % 2, :]
                if r and leaves_after(*ROUNDS[r - 1]):
                    wait_outputs_left(pe, ROUNDS[r - 1][0])
                if kind == "A":
                    rows = slice(HEAD * part, HEAD * part + HEAD)
                    for qi in range(2):
                        tile = 2 * i + qi
                        for s in range(1 if tile == 0 else 0, 2):
                            m = nc.tensor.matmul(acc[rows, O_BANK, tile * P:(tile + 1) * P],
                                                 v_new[:, tile - 1 + s, HEAD * part:HEAD * part + HEAD],
                                                 pt[:, (2 * qi + s) * P:(2 * qi + s + 1) * P],
                                                 start=s == (tile == 0), stop=s == 1)
                elif kind == "As":
                    for e in range(2):
                        rows = slice(HEAD * e, HEAD * e + HEAD)
                        nc.tensor.matmul(acc[rows, O_BANK, 0:DEC], v_past_a[:, rows], pt[:, e * DEC:(e + 1) * DEC],
                                         start=True, stop=False)
                        m = nc.tensor.matmul(acc[rows, O_BANK, 0:DEC], v_new[0:DEC, SEQ_TILES, rows],
                                             pt[0:DEC, P + e * DEC:P + (e + 1) * DEC], start=False, stop=True)
                elif kind == "B":
                    for j in range(i + 1):
                        m = nc.tensor.matmul(acc[:, O_BANK, i * P:(i + 1) * P], pt[:, j * P:(j + 1) * P],
                                             v_new[:, j, P * (t + 1):P * (t + 2)], start=j == 0, stop=j == i)
                else:
                    for j in range(SEQ_TILES):
                        nc.tensor.matmul(acc[0:DEC, O_BANK, 0:P], pt[:, j * DEC:(j + 1) * DEC],
                                         v_past_b[:, j, P * t:P * (t + 1)], start=j == 0, stop=False)
                    m = nc.tensor.matmul(acc[0:DEC, O_BANK, 0:P], pt[0:DEC, SEQ_TILES * DEC:TOK_TILES * DEC],
                                         v_new[0:DEC, SEQ_TILES, P * (t + 1):P * (t + 2)], start=False, stop=True)
                m.then_inc(o_done, 1)

            def heads_back(n):
                h = UNITS[n][1]
                wait_scores_banks(pe, n)
                pe.wait_ge(ob_ready, h + 1)
                bank = pair(n)
                for tt in range(SEQ_TILES):
                    nc.tensor.transpose(acc[:, bank, tt * P:(tt + 1) * P], o_b[:, h % 2, tt, :], ident[:])
                nc.tensor.transpose(acc[:, bank + 1, 0:DEC], o_b[0:DEC, h % 2, SEQ_TILES, :],
                                    ident[0:DEC, 0:DEC]).then_inc(ob_turned, 1)

            def out_step(d, k):
                bank = 2 * (d % 2)
                if k == 0:
                    block_ready(W_OUT + d)
                    if d >= 2:
                        pe.wait_ge(res_ready, KD + d - 1)
                    elif d == 0:
                        pe.wait_ge(x_out, len(TILES))
                    else:
                        pe.wait_ge(exp_done, len(score_order))
                        pe.wait_ge(mix_ready, mix_count[bank_order[-1]])
                if d == 0:
                    pe.wait_ge(mix_ready, max(c for n, c in mix_count.items() if mix_tile(n) == k))
                m = feature_products(bank, (W_OUT + d) % SPLIT_SLOTS, k, mix_hi, mix_lo, k, k == 0, k == KD - 1)
                if k == KD - 1:
                    m.then_inc(block_used, 1)

            for event in EVENTS:
                if event[0] == "k":
                    _, b, k = event
                    if b == len(TILES):
                        out_step(0, k)
                        continue
                    if k == 0:
                        block_ready(W_TILES + b)
                        if b == 0:
                            pe.wait_ge(v_out, 2 * TOK_TILES)
                            pe.wait_ge(rms_done, 3)
                        else:
                            pe.wait_ge(x_out, b)
                    m = feature_products(0, (W_TILES + b) % SPLIT_SLOTS, k, u_hi, u_lo, k, k == 0, k == KD - 1)
                    if k == KD - 1:
                        m.then_inc(block_used, 1)
                elif event[0] == "S":
                    scores(event[1])
                elif event[0] == "T":
                    transposes(event[1])
                elif event[0] == "O":
                    values(event[1])
                elif event[0] == "L":
                    heads_back(event[1])

            for d in range(1, KD):
                for k in range(KD):
                    out_step(d, k)

            ffn(W_FFN2, 1)
            norm_sums(3, NORM_BANK)

        @block.scalar
        def _(act):
            def hi_part(w, width, w_static):
                act.wait_ge(raw_in[w_static % RAW_SLOTS], 16 * arrivals(w, w_static))
                if w_static >= SPLIT_SLOTS:
                    act.wait_ge(block_used, w - SPLIT_SLOTS + 1)
                nc.scalar.activation(w_hi[w_static % SPLIT_SLOTS][:, 0:width],
                                     raw[w_static % RAW_SLOTS][:, 0:width], ACT.Copy).then_inc(hi_ready, 1)

            def arrivals(w, w_static):
                if isinstance(w, int):
                    return w // RAW_SLOTS + 1
                return w_static // RAW_SLOTS + 1 + w.iteration

            class Later:
                def __init__(self, first, i):
                    self.first, self.iteration = first, i

                def __sub__(self, n):
                    return self.first - n + 4 * self.iteration

            def square(d):
                act.wait_ge(ssq_added, square.before + d)
                nc.scalar.activation(sq[:], res[:, d, :], ACT.Square).then_inc(sq_ready, 1)

            def rms(count, bank):
                act.wait_ge(sum_done, count + 1)
                nc.scalar.activation(rrow[:, :].rearrange("p (t n) -> p t n", t=2), acc[:, bank:bank + 2, 0:HALF],
                                     ACT.Sqrt, scale=1.0 / D_MODEL, bias=eps[:, 0:1]).then_inc(rms_done, 1)

            def u_hi_part(norm, d):
                nc.scalar.activation(u_hi[:, d, :], res[:, d, :], ACT.Copy,
                                     scale=gains[:, norm, d:d + 1]).then_inc(uhi_ready, 1)

            def static_wait():
                act.wait_ge(gains_in, 16)

            act.wait_ge(gains_in, 16)
            act.wait_ge(set_up, 2)
            for d in range(KD):
                act.wait_ge(x_in[d // 4], 16)
                u_hi_part(0, d)
                if d == 0:
                    hi_part(0, block_width(0), 0)
                square.before = 0
                square(d)
                if d == 0:
                    hi_part(1, block_width(1), 1)

            def gate_up(base, i, ffn_no, last=False):
                for j in range(2):
                    for part in range(2):
                        q = 2 * j + part
                        w_static = base + q + 2
                        w = Later(w_static, i) if not isinstance(i, int) else w_static + 4 * i
                        width = block_width(w) if isinstance(w, int) else KD * P
                        hi_part(w, width, w_static)
                        if part == 0:
                            if isinstance(i, int) and i == 0 and j == 0:
                                rms(NORMS_BEFORE[ffn_no], NORM_BANK)
                            act.wait_ge(g_out, KF * ffn_no + 2 * i + j + 1)
                            nc.scalar.activation(gate[:], gate[:], ACT.Silu).then_inc(silu_done, 1)
                        else:
                            act.wait_ge(h_full, KF * ffn_no + 2 * i + j + 1)
                            static_wait()
                            nc.scalar.activation(h_hi[:, 2 * i + j, :], up[:], ACT.Copy).then_inc(hhi_ready, 1)

            def residual_next(norm, d, count):
                act.wait_ge(res_ready, count + d + 1)
                act.wait_ge(ssq_added, KD * norm + d)
                static_wait()
                if norm < 3:
                    nc.scalar.activation(u_hi[:, d, :], res[:, d, :], ACT.Copy,
                                         scale=gains[:, norm, bass.ds(d, 1)]).then_inc(uhi_ready, 1)
                nc.scalar.activation(sq[:], res[:, d, :], ACT.Square).then_inc(sq_ready, 1)

            def ffn(base, ffn_no):
                gate_up(base, 0, ffn_no)
                with act.Fori(1, KF // 2 - 1) as i:
                    gate_up(base, i, ffn_no)
                gate_up(base, KF // 2 - 1, ffn_no)
                down = base + 2 * KF

                def down_pair(i):
                    for j in range(2):
                        for c in range(2):
                            w_static = down + 2 * j + c + 2
                            w = Later(w_static, i) if not isinstance(i, int) else w_static + 4 * i
                            if not isinstance(w, int) or w < BLOCKS:
                                hi_part(w, block_width(w) if isinstance(w, int) else SLOT, w_static)
                        residual_next(2 * ffn_no + 1, 2 * i + j, DOWNS_BEFORE[ffn_no])
                with act.Fori(0, KD // 2 - 1) as i:
                    down_pair(i)
                down_pair(KD // 2 - 1)

            ffn(0, 0)

            for c in range(2):
                for kc in range(2):
                    w = W_V + 2 * c + kc
                    hi_part(w + 2, block_width(w + 2), w + 2)
                    if c == 0 and kc == 0:
                        rms(1, 2)
                        act.wait_ge(sum_done, 3)
                        nc.scalar.activation(r_tok[:, 0, 0:SEQ_TILES], acc[:, 1, 0:SEQ_TILES], ACT.Sqrt,
                                             scale=1.0 / D_MODEL, bias=eps[:, 0:1])
                        nc.scalar.activation(r_tok[0:DEC, 0, SEQ_TILES:TOK_TILES],
                                             acc[0:DEC, 1, SEQ_TILES:TOK_TILES], ACT.Sqrt,
                                             scale=1.0 / D_MODEL, bias=eps[0:DEC, 0:1]).then_inc(rms_done, 1)
                    if kc == 1:
                        for tt in range(TOK_TILES):
                            n_tok = P if tt < SEQ_TILES else DEC
                            if tt < TOK_TILES - 1:
                                act.wait_ge(v_done, (TOK_TILES - 1) * c + tt + 1)
                            else:
                                act.wait_ge(block_used, w + 1)
                            act.wait_ge(r_ready, 2)
                            nc.scalar.activation(v_new[0:n_tok, tt, c * V_HALF:(c + 1) * V_HALF],
                                                 acc[0:n_tok, V_BANK[tt], 0:V_HALF], ACT.Copy,
                                                 scale=r_tok[0:n_tok, 1, tt:tt + 1]).then_inc(v_out, 1)

            act.wait_ge(lam_sums, 2)
            nc.scalar.activation(lam[:, 2:4], lam[:, 0:2], ACT.Exp).then_inc(lam_exp, 1)

            def exps(n):
                kind, t, i = UNITS[n]
                sl = score_at[n]
                par = sl % 2
                act.wait_ge(max_ready, sl + 1)
                if sl >= 2:
                    act.wait_ge(turned_done, last_round[score_order[sl - 2]] + 1)
                bank = pair(n)
                pr = probs[:, par, :]
                if kind == "A":
                    nc.scalar.activation(st[:, par, 3, :], st[:, par, 2, :], ACT.Exp)
                    for s in range(4):
                        m = nc.scalar.activation(pr[:, 256 * s:256 * (s + 1)],
                                                 acc[:, bank + s // 2, 256 * (s % 2):256 * (s % 2 + 1)], ACT.Exp,
                                                 scale=SCALE, bias=st[:, par, 1, s:s + 1],
                                                 accum_out=st[:, par, 4, s:s + 1])
                elif kind == "As":
                    nc.scalar.activation(st[:, par, 3, 0:1], st[:, par, 2, 0:1], ACT.Exp)
                    m = nc.scalar.activation(pr[:, 0:A_PAST + DEC], acc[:, bank, 0:A_PAST + DEC], ACT.Exp,
                                             scale=SCALE, bias=st[:, par, 1, 0:1], accum_out=st[:, par, 4, 0:1])
                elif kind == "B":
                    for e in range(2):
                        m = nc.scalar.activation(pr[:, BANK * e:BANK * e + (i + 1) * P], acc[:, bank + e, 0:(i + 1) * P],
                                                 ACT.Exp, scale=SCALE, bias=st[:, par, 1, e:e + 1],
                                                 accum_out=st[:, par, 4, e:e + 1])
                else:
                    m = nc.scalar.activation(pr[:, 0:TOK].rearrange("p (c n) -> p c n", c=2),
                                             acc[:, bank:bank + 2, 0:HALF], ACT.Exp,
                                             scale=SCALE, bias=st[:, par, 1, 0:1], accum_out=st[:, par, 4, 0:1])
                m.then_inc(exp_done, 1)

            def copy_turned(r):
                n, part = ROUNDS[r]
                kind, t, i = UNITS[n]
                act.wait_ge(turned_done, r + 1)
                if r >= 2:
                    act.wait_ge(o_done, r - 1)
                pt = probs_t[:, r % 2, :]
                if kind == "As":
                    nc.scalar.activation(pt[:, 0:P], acc[:, T_BANK, 0:P], ACT.Copy)
                    m = nc.scalar.activation(pt[0:DEC, P:2 * P], acc[0:DEC, T_BANK, P:2 * P], ACT.Copy)
                elif kind == "Bs":
                    nc.scalar.activation(pt[:, 0:4 * DEC], acc[:, T_BANK, 0:4 * DEC], ACT.Copy)
                    m = nc.scalar.activation(pt[0:DEC, 4 * DEC:5 * DEC], acc[0:DEC, T_BANK, 4 * DEC:5 * DEC], ACT.Copy)
                else:
                    cols = slice(P if kind == "A" and i == 0 else 0, BANK if kind == "A" else (i + 1) * P)
                    m = nc.scalar.activation(pt[:, cols], acc[:, T_BANK, cols], ACT.Copy)
                m.then_inc(probs_t_ready, 1)

            def outputs(r):
                n, part = ROUNDS[r]
                kind, t, i = UNITS[n]
                if not leaves_after(n, part):
                    return
                act.wait_ge(o_done, r + 1)
                sample = kind[1:] == "s"
                if kind[0] == "A":
                    src = acc[:, O_BANK, 0:DEC] if sample else acc[:, O_BANK, :]
                    nc.scalar.activation(mix_hi[:, t, SEQ:TOK] if sample else mix_hi[:, t, 0:SEQ], src,
                                         ACT.Copy).then_inc(mixhi_ready, 1)
                else:
                    if t >= 2:
                        act.wait_ge(ob_turned, t - 1)
                    if t:
                        act.wait_ge(ss_ready, t)
                    if sample:
                        src, to = acc[0:DEC, O_BANK, 0:P], (slice(0, DEC), SEQ_TILES)
                    else:
                        src = acc[:, O_BANK, :].rearrange("p (t n) -> p t n", t=SEQ_TILES)
                        to = (slice(0, P), slice(0, SEQ_TILES))
                    nc.scalar.activation(o_b[to[0], t % 2, to[1], :], src, ACT.Copy)
                    nc.scalar.activation(sq_o[to[0], to[1], :], src, ACT.Square).then_inc(o_copied, 1)

            def root(n):
                h = UNITS[n][1]
                act.wait_ge(ss_ready, h + 1)
                nc.scalar.activation(ss_o[:, 1, h % 2, 0:TOK_TILES], ss_o[:, 0, h % 2, 0:TOK_TILES], ACT.Sqrt,
                                     scale=1.0 / P, bias=eps[:, 0:1]).then_inc(ss_root, 1)

            def mix_hi_b(n):
                h = UNITS[n][1]
                act.wait_ge(ob_turned, h + 1)
                act.wait_ge(coef_ready, 1)
                bank = pair(n)
                nc.scalar.activation(mix_hi[:, PAIRS + h, 0:SEQ], acc[:, bank, :], ACT.Copy, scale=lam[:, 6:7])
                nc.scalar.activation(mix_hi[:, PAIRS + h, SEQ:TOK], acc[:, bank + 1, 0:DEC], ACT.Copy,
                                     scale=lam[:, 6:7]).then_inc(mixhi_ready, 1)

            for event in EVENTS:
                if event[0] == "k" and event[2] == KD - 1 and event[1] < len(TILES):
                    w = W_TILES + event[1]
                    hi_part(w + 2, block_width(w + 2), w + 2)
                elif event[0] == "S":
                    exps(event[1])
                elif event[0] == "T":
                    copy_turned(event[1])
                elif event[0] == "O":
                    outputs(event[1])
                elif event[0] == "R":
                    root(event[1])
                elif event[0] == "L":
                    mix_hi_b(event[1])

            for d in range(KD):
                w = W_OUT + d
                hi_part(w + 2, block_width(w + 2), w + 2)
                residual_next(2, d, KD)
            ffn(W_FFN2, 1)
            rms(NORMS_BEFORE[1] + 1, NORM_BANK)

        @block.vector
        def _(dve):
            chain = [0]

            def then(ins):
                chain[0] += 1
                ins.then_inc(dv, 1)
                dve.wait_ge(dv, chain[0])

            def lo_part(w, width, w_static):
                dve.wait_ge(hi_ready, w + 1)
                nc.vector.tensor_tensor(w_lo[w_static % SPLIT_SLOTS][:, 0:width], raw[w_static % RAW_SLOTS][:, 0:width],
                                        w_hi[w_static % SPLIT_SLOTS][:, 0:width].bitcast(FP32),
                                        ALU.subtract).then_inc(split_ready, 1)

            def u_lo_part(norm, d):
                nc.vector.scalar_tensor_tensor(out=u_lo[:, d, :], in0=res[:, d, :], scalar=gains[:, norm, bass.ds(d, 1)],
                                               in1=u_hi[:, d, :].bitcast(FP32), op0=ALU.mult,
                                               op1=ALU.subtract).then_inc(u_ready, 1)

            nc.vector.memset(ones[:], 1.0).then_inc(set_up, 1)
            nc.vector.memset(eps[:], EPS).then_inc(set_up, 1)
            dve.wait_ge(gains_in, 16)
            for d in range(KD):
                dve.wait_ge(uhi_ready, d + 1)
                u_lo_part(0, d)
                if d < 2:
                    lo_part(d, block_width(d), d)

            def halves(t):
                return t.rearrange("p (t n) -> p t n", t=2)

            def gate_up(base, i, ffn_no):
                for j in range(2):
                    f = 2 * i + j
                    for part in range(2):
                        q = 2 * j + part
                        w = base + 4 * i + q + 2
                        lo_part(w, block_width(w) if isinstance(w, int) else KD * P, base + q + 2)
                        bank = 2 * q
                        dve.wait_ge(block_used, w - 1)
                        if part == 0:
                            if isinstance(i, int) and i == 0 and j == 0:
                                dve.wait_ge(rms_done, NORMS_BEFORE[ffn_no] + 1)
                                nc.vector.reciprocal(rrow[:], rrow[:]).then_inc(r_ready, 1)
                                dve.wait_ge(r_ready, NORMS_BEFORE[ffn_no] + 1)
                            nc.vector.tensor_tensor(halves(gate[:, :]), acc[:, bank:bank + 2, 0:HALF], halves(rrow[:, :]),
                                                    ALU.mult).then_inc(g_out, 1)
                        else:
                            nc.vector.tensor_tensor(halves(up[:, :]), acc[:, bank:bank + 2, 0:HALF], halves(rrow[:, :]),
                                                    ALU.mult).then_inc(u_out, 1)
                            dve.wait_ge(u_out, KF * ffn_no + f + 1)
                            dve.wait_ge(silu_done, KF * ffn_no + f + 1)
                            nc.vector.tensor_tensor(up[:], up[:], gate[:], ALU.mult).then_inc(h_full, 1)
                            dve.wait_ge(h_full, KF * ffn_no + f + 1)
                            dve.wait_ge(hhi_ready, KF * ffn_no + f + 1)
                            nc.vector.tensor_tensor(h_lo[:, f, :], up[:], h_hi[:, f, :].bitcast(FP32),
                                                    ALU.subtract).then_inc(h_ready, 1)

            def next_u(norm, d):
                dve.wait_ge(uhi_ready, norms_u(norm) + d + 1)
                u_lo_part(norm, d)

            def ffn(base, ffn_no):
                gate_up(base, 0, ffn_no)
                with dve.Fori(1, KF // 2 - 1) as i:
                    gate_up(base, i, ffn_no)
                gate_up(base, KF // 2 - 1, ffn_no)
                down = base + 2 * KF

                def down_pair(i):
                    for j in range(2):
                        d = 2 * i + j
                        for c in range(2):
                            w = down + 4 * i + 2 * j + c + 2
                            if not isinstance(w, int) or w < BLOCKS:
                                lo_part(w, block_width(w) if isinstance(w, int) else SLOT, down + 2 * j + c + 2)
                        dve.wait_ge(block_used, down + 4 * i + 2 * j + 2)
                        nc.vector.scalar_tensor_tensor(out=halves(res[:, d, :]), in0=acc[:, 2 * j:2 * j + 2, 0:HALF],
                                                       scalar=0.5, in1=halves(res[:, d, :]), op0=ALU.mult,
                                                       op1=ALU.add).then_inc(res_ready, 1)
                        if ffn_no == 0:
                            next_u(1, d)
                with dve.Fori(0, KD // 2 - 1) as i:
                    down_pair(i)
                down_pair(KD // 2 - 1)

            ffn(0, 0)

            for c in range(2):
                for kc in range(2):
                    w = W_V + 2 * c + kc
                    lo_part(w + 2, block_width(w + 2), w + 2)
                    if c == 0 and kc == 0:
                        dve.wait_ge(rms_done, 3)
                        nc.vector.reciprocal(r_tok[:, 1, 0:SEQ_TILES], r_tok[:, 0, 0:SEQ_TILES])
                        nc.vector.reciprocal(r_tok[0:DEC, 1, SEQ_TILES:TOK_TILES],
                                             r_tok[0:DEC, 0, SEQ_TILES:TOK_TILES]).then_inc(r_ready, 1)
                        nc.vector.reciprocal(rrow[:], rrow[:]).then_inc(r_ready, 1)
                        dve.wait_ge(consts_in, 48)
                        for e in range(2):
                            nc.vector.tensor_tensor_reduce(out=sq_o[:, e, 0:HEAD], in0=lvec[:, 2 * e, :],
                                                           in1=lvec[:, 2 * e + 1, :], scale=1.0, scalar=0.0,
                                                           op0=ALU.mult, op1=ALU.add,
                                                           accum_out=lam[:, e:e + 1]).then_inc(lam_sums, 1)
                        then(nc.vector.tensor_tensor(ident2[:], ident[:, 0:DEC], ident[:, DEC:2 * DEC], ALU.add))
                        dve.wait_ge(lam_sums, 2)
                        nc.vector.memset(sq_o[:], 1.0)
                        then(nc.vector.memset(o_b[:], 0.0))
            dve.wait_ge(lam_exp, 1)
            then(nc.vector.tensor_tensor(lam[:, 4:5], lam[:, 3:4], lam[:, 2:3], ALU.subtract))
            then(nc.vector.tensor_scalar(lam[:, 4:5], lam[:, 4:5], -LAM_INIT, None, ALU.add))
            nc.vector.memset(lam[0:HEAD, 5:6], 1.0)
            nc.vector.tensor_copy(lam[HEAD:P, 5:6], lam[HEAD:P, 4:5])
            then(nc.vector.tensor_scalar(lam[:, 6:7], gsub, 1.0 - LAM_INIT, None, ALU.mult))
            nc.vector.tensor_copy(lam[:, 7:8], lam[:, 6:7]).then_inc(coef_ready, 1)

            def take_projection(b):
                dve.wait_ge(block_used, W_TILES + b + 1)
                if b == 0:
                    dve.wait_ge(trig_ready, 2)
                else:
                    dve.wait_ge(rope_done, b)
                nc.vector.stream_shuffle(halves(turned[:, :]), acc[:, 0:2, 0:HALF],
                                         [(i + 16) % 32 for i in range(32)]).then_inc(turn_done, 1)
                nc.vector.tensor_tensor(halves(rope_x[:, :]), acc[:, 0:2, 0:HALF], halves(trig_r[:, 0, :]),
                                        ALU.mult).then_inc(x_out, 1)

            def maxima(n):
                kind, t, i = UNITS[n]
                sl = score_at[n]
                par = sl % 2
                bank = pair(n)
                s = st[:, par]
                dve.wait_ge(scores_done, sl + 1)
                if kind == "A":
                    v = acc[:, bank:bank + 2, :].rearrange("p b (q n) -> p (b q) n", q=2)
                    nc.vector.memset(v[0:CHUNK, :, 192:256], NEG)
                    if i == 0:
                        nc.vector.memset(acc[:, bank:bank + 2, 0:P], NEG)
                        then(nc.vector.memset(acc[CHUNK:P, bank:bank + 2, 256:256 + CHUNK], NEG))
                    else:
                        then(nc.vector.memset(v[CHUNK:P, :, 0:CHUNK], NEG))
                    then(nc.vector.reduce_max(s[:, 0, 0:4], v, AX.X))
                    cols, sink = slice(0, 4), sink_p[:, t, :]
                elif kind == "As":
                    then(nc.vector.reduce_max(s[:, 0, 0:1], acc[:, bank, 0:A_PAST + DEC], AX.X))
                    cols, sink = slice(0, 1), sink_s[:, t:t + 1]
                elif kind == "B":
                    then(nc.vector.memset(acc[0:CHUNK, bank:bank + 2, i * P + CHUNK:(i + 1) * P], NEG))
                    then(nc.vector.reduce_max(s[:, 0, 0:2], acc[:, bank:bank + 2, 0:(i + 1) * P], AX.X))
                else:
                    then(nc.vector.reduce_max(s[:, 0, 0:1], acc[:, bank:bank + 2, 0:HALF], AX.XY))
                if kind[0] == "A":
                    then(nc.vector.scalar_tensor_tensor(out=s[:, 0, cols], in0=s[:, 0, cols], scalar=SCALE, in1=sink,
                                                        op0=ALU.mult, op1=ALU.max))
                    nc.vector.tensor_scalar(s[:, 1, cols], s[:, 0, cols], -1.0, None, ALU.mult)
                    nc.vector.tensor_tensor(s[:, 2, cols], sink, s[:, 0, cols], ALU.subtract).then_inc(max_ready, 1)
                else:
                    cols = slice(0, 2 if kind == "B" else 1)
                    nc.vector.tensor_scalar(s[:, 1, cols], s[:, 0, cols], -SCALE, None, ALU.mult).then_inc(max_ready, 1)

            def normalise(n):
                kind, t, i = UNITS[n]
                sl = score_at[n]
                par = sl % 2
                s = st[:, par]
                pr = probs[:, par, :]
                dve.wait_ge(exp_done, sl + 1)
                cols = slice(0, {"A": 4, "As": 1, "B": 2, "Bs": 1}[kind])
                if kind[0] == "A":
                    then(nc.vector.tensor_tensor(s[:, 4, cols], s[:, 4, cols], s[:, 3, cols], ALU.add))
                then(nc.vector.reciprocal(s[:, 5, cols], s[:, 4, cols]))
                if kind == "A":
                    for q in range(4):
                        m = nc.vector.tensor_scalar(pr[:, 256 * q:256 * (q + 1)], pr[:, 256 * q:256 * (q + 1)],
                                                    s[:, 5, q:q + 1], None, ALU.mult)
                elif kind == "As":
                    m = nc.vector.tensor_scalar(pr[:, 0:A_PAST + DEC], pr[:, 0:A_PAST + DEC], s[:, 5, 0:1], None, ALU.mult)
                elif kind == "B":
                    nc.vector.tensor_tensor(s[:, 6, 0:1], s[:, 5, 1:2], lam[:, 4:5], ALU.mult)
                    w = (i + 1) * P
                    then(nc.vector.tensor_scalar(pr[:, 0:w], pr[:, 0:w], s[:, 5, 0:1], None, ALU.mult))
                    m = nc.vector.scalar_tensor_tensor(out=pr[:, 0:w], in0=pr[:, BANK:BANK + w], scalar=s[:, 6, 0:1],
                                                       in1=pr[:, 0:w], op0=ALU.mult, op1=ALU.add)
                else:
                    then(nc.vector.tensor_tensor(s[:, 6, 0:1], s[:, 5, 0:1], lam[:, 5:6], ALU.mult))
                    if t:
                        dve.wait_ge(turned_done, last_round[units_bs[t - 1]] + 1)
                    m = nc.vector.tensor_scalar(diag[:], ident2[:], s[:, 6, 0:1], None, ALU.mult)
                m.then_inc(probs_ready, 1)

            def outputs(r):
                n, part = ROUNDS[r]
                kind, t, i = UNITS[n]
                if not leaves_after(n, part):
                    return
                sample = kind[1:] == "s"
                if kind[0] == "A":
                    dve.wait_ge(mixhi_ready, mix_count[n])
                    to = slice(SEQ, TOK) if sample else slice(0, SEQ)
                    src = acc[:, O_BANK, 0:DEC] if sample else acc[:, O_BANK, :]
                    nc.vector.tensor_tensor(mix_lo[:, t, to], src, mix_hi[:, t, to].bitcast(FP32),
                                            ALU.subtract).then_inc(mix_ready, 1)
                elif not sample:
                    dve.wait_ge(o_copied, copy_count[n])
                    nc.vector.tensor_reduce(ss_o[:, 0, t % 2, 0:TOK_TILES], sq_o[:], AX.X,
                                            ALU.add).then_inc(ss_ready, 1)

            def head_norm(n):
                h = UNITS[n][1]
                dve.wait_ge(ss_root, h + 1)
                then(nc.vector.reciprocal(ss_o[:, 2, h % 2, 0:TOK_TILES], ss_o[:, 1, h % 2, 0:TOK_TILES]))
                for tt in range(TOK_TILES):
                    m = nc.vector.tensor_scalar(o_b[:, h % 2, tt, :], o_b[:, h % 2, tt, :],
                                                ss_o[:, 2, h % 2, tt:tt + 1], None, ALU.mult)
                m.then_inc(ob_ready, 1)

            def heads_back(n):
                h = UNITS[n][1]
                bank = pair(n)
                dve.wait_ge(mixhi_ready, mix_count[n])
                nc.vector.scalar_tensor_tensor(out=mix_lo[:, PAIRS + h, 0:SEQ], in0=acc[:, bank, :], scalar=lam[:, 6:7],
                                               in1=mix_hi[:, PAIRS + h, 0:SEQ].bitcast(FP32), op0=ALU.mult,
                                               op1=ALU.subtract)
                nc.vector.scalar_tensor_tensor(out=mix_lo[:, PAIRS + h, SEQ:TOK], in0=acc[:, bank + 1, 0:DEC],
                                               scalar=lam[:, 6:7], in1=mix_hi[:, PAIRS + h, SEQ:TOK].bitcast(FP32),
                                               op0=ALU.mult, op1=ALU.subtract).then_inc(mix_ready, 1)

            for event in EVENTS:
                if event[0] == "k" and event[2] == KD - 1 and event[1] < len(TILES):
                    take_projection(event[1])
                    w = W_TILES + event[1]
                    lo_part(w + 2, block_width(w + 2), w + 2)
                elif event[0] == "S":
                    maxima(event[1])
                elif event[0] == "N":
                    normalise(event[1])
                elif event[0] == "O":
                    outputs(event[1])
                elif event[0] == "R":
                    head_norm(event[1])
                elif event[0] == "L":
                    heads_back(event[1])

            for d in range(KD):
                w = W_OUT + d
                lo_part(w + 2, block_width(w + 2), w + 2)
                dve.wait_ge(block_used, w + 1)
                bank = 2 * (d % 2)
                nc.vector.tensor_tensor(halves(res[:, d, :]), acc[:, bank:bank + 2, 0:HALF], halves(res[:, d, :]),
                                        ALU.add).then_inc(res_ready, 1)
                next_u(2, d)
            dve.wait_ge(kv_stored, KV_STORES)
            for h in range(B_HEADS):
                dve.wait_ge(k_stored[h], 16)
            ffn(W_FFN2, 1)

            dve.wait_ge(rms_done, NORMS_BEFORE[1] + 2)
            nc.vector.reciprocal(rrow[:], rrow[:]).then_inc(r_ready, 1)
            dve.wait_ge(r_ready, NORMS_BEFORE[1] + 2)
            for d in range(KD):
                nc.vector.scalar_tensor_tensor(out=res[:, d, :], in0=res[:, d, :], scalar=gains[:, 3, d:d + 1],
                                               in1=rrow[:], op0=ALU.mult, op1=ALU.mult).then_inc(y_ready, 1)

        @block.gpsimd
        def _(gp):
            steps = [0]

            def then(ins):
                steps[0] += 1
                ins.then_inc(gp_step, 1)
                gp.wait_ge(gp_step, steps[0])

            def sums(norm, times, loop=False):
                if norm:
                    gp.wait_ge(sum_done, SUMS_BEFORE[norm])
                nc.gpsimd.memset(ssq[:], 0.0).then_inc(ssq_zero, 1)
                gp.wait_ge(ssq_zero, norm + 1)
                with gp.Fori(0, KD) as d:
                    gp.wait_ge(sq_ready, KD * norm + d + 1)
                    gp.wait_ge(ssq_added, KD * norm + d)
                    nc.gpsimd.tensor_tensor(ssq[:], ssq[:], sq[:], ALU.add).then_inc(ssq_added, 1)

            sums(0, KD)
            sums(1, KD)
            gp.wait_ge(block_used, FFN_BLOCKS)
            nc.gpsimd.memset(q_diag[:], 0.0).then_inc(zeroed, 1)
            gp.wait_ge(r_ready, 3)
            gp.wait_ge(consts_in, 48)
            for c in range(2):
                nc.gpsimd.tensor_tensor(trig_r[:, c, :], trig[:, c, :], rrow[:], ALU.mult).then_inc(trig_ready, 1)
            gp.wait_ge(trig_ready, 2)
            gp.wait_ge(zeroed, 1)

            for b, name in enumerate(TILES):
                gp.wait_ge(turn_done, b + 1)
                then(nc.gpsimd.tensor_tensor(turned[:], turned[:], trig_r[:, 1, :], ALU.mult))
                gp.wait_ge(x_out, b + 1)
                if name == "ka":
                    nc.gpsimd.tensor_tensor(k_a[:], rope_x[:, 0:SEQ], turned[:, 0:SEQ], ALU.add)
                    m = nc.gpsimd.tensor_tensor(k_all_a[:, A_PAST:A_PAST + DEC], rope_x[:, SEQ:TOK],
                                                turned[:, SEQ:TOK], ALU.add)
                else:
                    slot = int(name[2]) % 2
                    former = [n for c in range(b) if TILES[c][0:2] == name[0:2] and int(TILES[c][2]) % 2 == slot
                              for n in tile_users(c)]
                    if former:
                        gp.wait_ge(scores_done, max(score_at[n] for n in former) + 1)
                    if name[0] == "k":
                        if int(name[2]) >= 2:
                            gp.wait_ge(k_stored[int(name[2]) - 2], 16)
                        nc.gpsimd.tensor_tensor(k_b[:, slot, :], rope_x[:, 0:SEQ], turned[:, 0:SEQ], ALU.add)
                        m = nc.gpsimd.tensor_tensor(k_all_b[:, int(name[2]), PAST:PAST + DEC], rope_x[:, SEQ:TOK],
                                                    turned[:, SEQ:TOK], ALU.add)
                    else:
                        dst = q_a if name[1] == "a" else q_b
                        then(nc.gpsimd.tensor_tensor(dst[:, slot, :], rope_x[:, 0:SEQ], turned[:, 0:SEQ], ALU.add))
                        before = [n for c in range(b) if TILES[c][0] == "q" and c % 2 == b % 2
                                  for n in tile_users(c) if UNITS[n][0][1:] == "s"]
                        if before:
                            gp.wait_ge(scores_done, max(score_at[n] for n in before) + 1)
                        for e in range(2):
                            rows = slice(HEAD * e, HEAD * e + HEAD)
                            m = nc.gpsimd.tensor_tensor(q_diag[rows, b % 2, rows], rope_x[rows, SEQ:TOK],
                                                        turned[rows, SEQ:TOK], ALU.add)
                            if e == 0:
                                then(m)
                m.then_inc(rope_done, 1)
                gp.wait_ge(rope_done, b + 1)
            sums(2, KD)
            sums(3, KD)


KV_STORES = 16 * 8
NORMS_BEFORE = (0, 3)
SUMS_BEFORE = (0, 1, 3, 4)
DOWNS_BEFORE = (0, 2 * KD)
last_round = {u: r for r, (u, _) in enumerate(ROUNDS)}
units_bs = [n for n, u in enumerate(UNITS) if u[0] == "Bs"]

HEAD_ORDER = np.concatenate([np.arange(0, 16), np.arange(32, 48), np.arange(16, 32), np.arange(48, 64)])


def kernel(**inputs):
    import concourse.bacc as bacc
    from concourse.bass_utils import run_bass_kernel_spmd

    x = {k: np.ascontiguousarray(v) for k, v in inputs.items()}
    f32 = np.float32

    def tiled(w, cols):
        k, n = w.shape
        return w.reshape(k // P, P, n // cols, cols).transpose(2, 1, 0, 3).reshape(n // cols, P, -1)

    def gate_up(g, u):
        return np.stack([tiled(g, P), tiled(u, P)], axis=2)

    def down(w):
        t = tiled(w, P).reshape(KD, P, 2, -1)
        return t

    def per_partition(v):
        return v.reshape(-1, P).T

    xt = np.concatenate([x["x_prompt"][0], x["x_sample"][0]], axis=0)
    xt = xt.T.reshape(KD, P, TOK).transpose(1, 0, 2)

    w_in = x["w_in"][0]
    cuts = np.cumsum([512, 128, 128, 512, 512])
    wqa, wka, wva, wqb, wkb, wvb = np.split(w_in, cuts, axis=1)

    def head_cols(w, heads):
        return np.concatenate([w[:, h * HEAD + HEAD_ORDER] for h in heads], axis=1)

    groups = [head_cols(wka, (0, 1))] + [head_cols(wqa, (t, t + PAIRS)) for t in range(PAIRS)]
    for h in range(B_HEADS):
        groups += [head_cols(wkb, (2 * h, 2 * h + 1)), head_cols(wqb, (2 * h, 2 * h + 1))]
    w_qk = np.concatenate([tiled(g, P) for g in groups], axis=0)
    w_v = np.concatenate([wva, wvb], axis=1)
    w_v = np.stack([tiled(w_v[512 * kc:512 * (kc + 1)], V_HALF)[c] for c in range(2) for kc in range(2)])
    rows = np.concatenate([np.r_[t * HEAD:(t + 1) * HEAD, (t + PAIRS) * HEAD:(t + PAIRS + 1) * HEAD]
                           for t in range(PAIRS)] + [np.arange(512, 1024)])
    w_out = tiled(x["w_out"][0][rows], P)

    def keys(c, heads):
        c = c[:, :, HEAD_ORDER]
        return c.transpose(1, 2, 0).reshape(heads // 2, P, -1)

    pos = np.arange(TOK).astype(f32)
    inv = (10000.0 ** (-np.arange(32) / 32.0)).astype(f32)
    ang = (pos[None, :] * inv[:, None]).astype(np.float64)
    dims = np.tile(HEAD_ORDER, 2)
    trig = np.stack([np.cos(ang)[dims % 32], np.sin(ang)[dims % 32] * np.where(dims < 32, -1.0, 1.0)[:, None]],
                    axis=1).astype(f32)
    sinks = x["attn_sinks"][0]
    sink_p = np.stack([sinks[[t, t, t + PAIRS, t + PAIRS]] for t in range(PAIRS)]).reshape(1, 16)
    sink_s = np.concatenate([np.tile(sinks[0:4], (HEAD, 1)), np.tile(sinks[4:8], (HEAD, 1))], axis=0)
    lam = np.concatenate([x[n][0] for n in ("lambda_q1", "lambda_k1", "lambda_q2", "lambda_k2")])[None]
    small = np.concatenate([np.tile(sink_p, (P, 1)), sink_s, x["subln_norm"][0][:, None], np.tile(lam, (P, 1))], axis=1)
    gains = np.stack([per_partition(x[n].reshape(-1)) for n in ("ffn1_norm", "mix_norm", "ffn2_norm", "final_norm")],
                     axis=1)
    arrays = {
        "gains": gains, "x": xt,
        "w1gu": gate_up(x["ffn1_w_gate"][0], x["ffn1_w_up"][0]), "w1d": down(x["ffn1_w_down"][0]),
        "w2gu": gate_up(x["ffn2_w_gate"][0], x["ffn2_w_up"][0]), "w2d": down(x["ffn2_w_down"][0]),
        "w_v": w_v, "w_qk": w_qk, "w_out": w_out,
        "ident": np.eye(P, dtype=f32), "trig": trig, "small": small,
        "k_past_a": keys(x["cache_a_k"][0, 0], 2)[0], "v_past_a": x["cache_a_v"][0, 0].reshape(A_PAST, P),
        "k_past_b": keys(x["cache_b_k"][0, 0], 8).transpose(1, 0, 2),
        "v_past_b": x["cache_b_v"][0, 0].reshape(SEQ_TILES, P, 512).transpose(1, 0, 2),
    }
    arrays = {k: np.ascontiguousarray(v) for k, v in arrays.items()}
    outs = {
        "y": (P, KD, TOK), "ak_p": (P, A_PAST), "av_p": (A_PAST, P), "bk_p": (B_HEADS, P, SEQ),
        "bv_p": (P, SEQ_TILES, 512), "ak_s": (P, A_PAST), "av_s": (A_PAST, P), "bk_s": (P, B_HEADS, DEC),
        "bv_s": (DEC, 512),
    }
    nc = bacc.Bacc("TRN2", target_bir_lowering=False, num_devices=1, dynamic_dma_scratch_size=1024)
    a = {k: nc.dram_tensor(f"in_{k}", v.shape, mybir.dt.from_np(v.dtype), kind="ExternalInput").ap()
         for k, v in arrays.items()}
    o = {k: nc.dram_tensor(f"out_{k}", s, FP32, kind="ExternalOutput").ap() for k, s in outs.items()}
    hybrid_step(nc, a, o)
    r = run_bass_kernel_spmd(nc, [{f"in_{k}": v for k, v in arrays.items()}], core_ids=[0])
    g = {k: np.asarray(r.results[0][f"out_{k}"]) for k in outs}

    back = np.argsort(HEAD_ORDER)

    def keys_back(k, heads):
        return k.reshape(heads, HEAD, -1)[:, back].transpose(2, 0, 1)

    y = g["y"].transpose(1, 0, 2).reshape(D_MODEL, TOK).T
    return (
        y[None, :SEQ], y[None, SEQ:],
        keys_back(g["ak_p"], 2)[None, None], g["av_p"].reshape(1, 1, A_PAST, 2, HEAD),
        keys_back(g["bk_p"], 8)[None, None],
        g["bv_p"].transpose(1, 0, 2).reshape(1, 1, SEQ, B_HEADS, P),
        keys_back(g["ak_s"], 2)[None, None], g["av_s"].reshape(1, 1, A_PAST, 2, HEAD),
        keys_back(g["bk_s"].transpose(1, 0, 2), 8)[None, None], g["bv_s"].reshape(1, 1, DEC, B_HEADS, P),
    )
```

```python
import concourse.bass as bass
import numpy as np
from concourse import mybir
from contextlib import ExitStack

FP32 = mybir.dt.float32
FP32R = mybir.dt.float32r
ALU = mybir.AluOpType
ACT = mybir.ActivationFunctionType
AX = mybir.AxisListType

P = 128
D_MODEL, D_FF = 1024, 2816
SEQ, DEC = 512, 64
TOK = SEQ + DEC
HALF = TOK // 2
CHUNK, HEAD = 64, 64
PAST, A_PAST = 512, 128
KD = D_MODEL // P
KF = D_FF // P
KF_HALF = KF // 2
PAIRS = 4
B_HEADS = 4
SEQ_TILES = SEQ // P
TOK_TILES = SEQ_TILES + 1
V_COLS = 640
V_HALF = V_COLS // 2
V_K = KD // 2
SLOT = KF_HALF * P
RAW_SLOTS, SPLIT_SLOTS = 4, 2
EPS = 1e-6
NEG = -1e30
SCALE = HEAD ** -0.5
LAM_INIT = 0.2
BANK = 512

TILES = ["ka", "qa0", "qa1", "qa2", "qa3"] + [f"{n}b{h}" for h in range(B_HEADS) for n in "kq"]
FILL_START, FILL_A, FILL_B, LEAD = 3, (2, 2, 2, 2.5), (3.2, 3.2, 3.2, 3.2), 2
V_BLOCKS = 4
FFN_BLOCKS = 2 * KF + 2 * KD
W_V = FFN_BLOCKS
W_TILES = W_V + V_BLOCKS
W_OUT = W_TILES + len(TILES)
W_FFN2 = W_OUT + KD
BLOCKS = W_FFN2 + FFN_BLOCKS
WARM_UP = 12
Y_GP = 2


def block_width(w):
    if W_V <= w < W_TILES:
        return V_K * V_HALF
    for first in (0, W_FFN2):
        if first + 2 * KF <= w < first + FFN_BLOCKS:
            return KF_HALF * P
    return KD * P


def make_schedule():
    units, rounds = [], []
    for t in range(PAIRS):
        units += [("A", t, 0), ("A", t, 1), ("As", t, 0)]
    for h in range(B_HEADS):
        units += [("Bs", h, 0)] + [("B", h, i) for i in range(SEQ_TILES)] + [("L", h, 0)]
    events, done, owed, ended = [], [0], [0], [False]
    steps = (len(TILES) + 1) * KD - 1

    def step():
        heads = sum(e[0] == "L" for e in events)
        if done[0] >= min(steps, len(TILES) * KD + PAIRS + heads):
            return False
        events.append(("k", done[0] // KD, done[0] % KD))
        done[0] += 1
        return True

    def fill(n):
        owed[0] += n
        if events[-1][0] != "k" and ended[0]:
            ended[0] = False
            return
        while owed[0] >= 1 and step():
            owed[0] -= 1
            if done[0] % KD == 0:
                ended[0] = True
                break

    def score(n):
        kind, t, _ = units[n]
        last = TILES.index(f"qa{t}" if kind[0] == "A" else f"qb{t}")
        while done[0] < (last + 1) * KD + LEAD and step():
            owed[0] = max(owed[0] - 1, 0)
        events.append(("S", n))

    scored = [n for n, u in enumerate(units) if u[0] != "L"]
    score(0)
    fill(FILL_START)
    score(1)
    events.append(("N", 0))
    fill(FILL_START)
    owed[0] = 1
    waiting = []
    for at, n in enumerate(scored):
        kind, head, i = units[n]
        parts = 2 if kind == "A" else 1
        for part in range(parts):
            r = len(rounds)
            rounds.append((n, part))
            events.append(("T", r))
            rate = FILL_A[head] if kind[0] == "A" else FILL_B[head]
            if part == parts - 1:
                if at + 1 < len(scored):
                    events.append(("N", scored[at + 1]))
                if at + 2 < len(scored):
                    score(scored[at + 2])
                fill(rate / 2)
            else:
                fill(max(1, rate / 2))
            events.append(("O", r))
            fill(rate / 2)
            waiting = [(e, m, k - 1) for e, m, k in waiting]
            while waiting and waiting[0][2] == 0:
                e, m, _ = waiting.pop(0)
                events.append((e, m))
        if kind == "B" and i == SEQ_TILES - 1:
            waiting += [("R", n + 1, 1), ("L", n + 1, 2)]
    while step():
        pass
    events += [(e, m) for e, m, _ in waiting]
    events.append(("k", len(TILES), KD - 1))
    return units, rounds, events


UNITS, ROUNDS, EVENTS = make_schedule()


def leaves_after(n, part):
    kind, _, i = UNITS[n]
    return kind[1:] == "s" or (kind == "A" and i == 1 and part == 1) or (kind == "B" and i == SEQ_TILES - 1)


def hybrid_step(nc, a, o):
    stack = ExitStack()
    with stack:
        def sb(name, shape, dt=FP32, where=stack):
            return where.enter_context(nc.sbuf_tensor(name, shape, dt))

        def sem(name):
            return stack.enter_context(nc.semaphore(name))

        res = sb("res", [P, KD, TOK])
        u_hi = sb("u_hi", [P, KD, TOK], FP32R)
        u_lo = sb("u_lo", [P, KD, TOK], FP32R)
        raw = [sb(f"raw{s}", [P, SLOT]) for s in range(RAW_SLOTS)]
        w_hi = [sb(f"w_hi{s}", [P, SLOT], FP32R) for s in range(SPLIT_SLOTS)]
        w_lo = [sb(f"w_lo{s}", [P, SLOT], FP32R) for s in range(SPLIT_SLOTS)]
        rrow = sb("rrow", [P, TOK])
        sq = sb("sq", [P, TOK])
        ssq = sb("ssq", [P, TOK])
        ones = sb("ones", [P, P])
        eps = sb("eps", [P, 1])
        gains = sb("gains", [P, 4, KD])
        with ExitStack() as ffn_mem:
            h_hi = sb("h_hi", [P, KF, TOK], FP32R, ffn_mem)
            h_lo = sb("h_lo", [P, KF, TOK], FP32R, ffn_mem)
            gate = sb("gate", [P, TOK], FP32, ffn_mem)
            up = sb("up", [P, TOK], FP32, ffn_mem)
        with ExitStack() as att_mem:
            def am(name, shape, dt=FP32):
                return sb(name, shape, dt, att_mem)
            ident = am("ident", [P, P])
            ident2 = am("ident2", [P, DEC])
            trig = am("trig", [P, 2, TOK])
            trig_r = am("trig_r", [P, 2, TOK])
            small = am("small", [P, 16 + 4 + 1 + 4 * HEAD])
            v_new = am("v_new", [P, TOK_TILES, V_COLS])
            v_past_b = am("v_past_b", [P, SEQ_TILES, BANK])
            v_past_a = am("v_past_a", [P, P])
            k_all_b = am("k_all_b", [P, B_HEADS, PAST + DEC])
            k_all_a = am("k_all_a", [P, A_PAST + DEC])
            k_a = am("k_a", [P, SEQ])
            q_a = am("q_a", [P, 2, SEQ])
            k_b = am("k_b", [P, 2, SEQ])
            q_b = am("q_b", [P, 2, SEQ])
            q_diag = am("q_diag", [P, 2, P])
            turned = am("turned", [P, TOK])
            rope_x = am("rope_x", [P, TOK])
            probs = am("probs", [P, 2, 2 * BANK])
            probs_t = am("probs_t", [P, 2, BANK])
            o_b = am("o_b", [P, 2, TOK_TILES, P])
            sq_o = am("sq_o", [P, TOK_TILES, P])
            diag = am("diag", [P, DEC])
            st = am("st", [P, 2, 8, 4])
            ss_o = am("ss_o", [P, 3, 2, 8])
            r_tok = am("r_tok", [P, 2, 8])
            lam = am("lam", [P, 8])
            mix_hi = am("mix_hi", [P, KD, TOK], FP32R)
            mix_lo = am("mix_lo", [P, KD, TOK], FP32R)
        sink_p = small[:, 0:16].rearrange("p (t n) -> p t n", t=PAIRS)
        sink_s = small[:, 16:20]
        gsub = small[:, 20:21]
        lvec = small[:, 21:21 + 4 * HEAD].rearrange("p (n d) -> p n d", n=4)

        acc = stack.enter_context(nc.psum_tensor("acc", [P, 8, BANK], FP32))
        NORM_BANK, FINAL_BANK = 6, 4

        x_in = [sem(f"x_in{i}") for i in range(KD // 2)]
        gains_in = sem("gains_in")
        consts_in = sem("consts_in")
        cache_in = sem("cache_in")
        raw_in = [sem(f"raw_in{s}") for s in range(RAW_SLOTS)]
        hi_ready = sem("hi_ready")
        split_ready = sem("split_ready")
        block_used = sem("block_used")
        set_up = sem("set_up")
        ssq_zero = sem("ssq_zero")
        sq_ready = sem("sq_ready")
        ssq_added = sem("ssq_added")
        uhi_ready = sem("uhi_ready")
        u_ready = sem("u_ready")
        res_ready = sem("res_ready")
        sum_done = sem("sum_done")
        rms_done = sem("rms_done")
        r_ready = sem("r_ready")
        g_out = sem("g_out")
        silu_done = sem("silu_done")
        u_out = sem("u_out")
        h_full = sem("h_full")
        hhi_ready = sem("hhi_ready")
        h_ready = sem("h_ready")
        v_done = sem("v_done")
        v_out = sem("v_out")
        trig_ready = sem("trig_ready")
        turn_done = sem("turn_done")
        x_out = sem("x_out")
        gp_step = sem("gp_step")
        rope_done = sem("rope_done")
        zeroed = sem("zeroed")
        dv = sem("dv")
        lam_sums = sem("lam_sums")
        lam_exp = sem("lam_exp")
        coef_ready = sem("coef_ready")
        scores_done = sem("scores_done")
        max_ready = sem("max_ready")
        exp_done = sem("exp_done")
        probs_ready = sem("probs_ready")
        turned_done = sem("turned_done")
        probs_t_ready = sem("probs_t_ready")
        o_done = sem("o_done")
        o_copied = sem("o_copied")
        o_squared = sem("o_squared")
        ss_ready = sem("ss_ready")
        ss_root = sem("ss_root")
        ob_ready = sem("ob_ready")
        ob_turned = sem("ob_turned")
        mixhi_ready = sem("mixhi_ready")
        mix_ready = sem("mix_ready")
        kv_stored = sem("kv_stored")
        k_stored = [sem(f"k_stored{h}") for h in range(B_HEADS)]
        last_half = sem("last_half")
        last_sq = sem("last_sq")
        y_scaled = sem("y_scaled")
        final_r = sem("final_r")
        y_ready = sem("y_ready")
        y_gp = sem("y_gp")
        y_stored = sem("y_stored")

        block = stack.enter_context(nc.Block())

        def norms_u(phase):
            return KD * phase

        T_BANK, O_BANK = 6, 7
        V_BANK = [4, 5, 6, 7, 3]
        TOK_SUM_BANK = 2

        def tile_bank(b):
            return T_BANK if b == 1 else 0

        def tile_users(b):
            name = TILES[b]
            return [n for n, u in enumerate(UNITS) if u[0] != "L" and (
                name == "ka" and u[0][0] == "A" or name == f"qa{u[1]}" and u[0][0] == "A"
                or name[1] == "b" and int(name[2]) == u[1] and u[0][0] == "B")]

        score_order = [n for e, n, *_ in EVENTS if e == "S"]
        l_order = [n for e, n, *_ in EVENTS if e == "L"]
        bank_order = [n for e, n, *_ in EVENTS if e in "SL"]
        order_at = {n: i for i, n in enumerate(bank_order)}
        score_at = {n: i for i, n in enumerate(score_order)}
        leaves = [ROUNDS[e[1]][0] for e in EVENTS if e[0] == "O" and leaves_after(*ROUNDS[e[1]])]
        pieces = [n for e, n in ((e[0], ROUNDS[e[1]][0] if e[0] == "O" else e[1]) for e in EVENTS
                                 if e[0] == "L" or e[0] == "O" and leaves_after(*ROUNDS[e[1]]))
                  if e == "L" or UNITS[n][0][0] == "A"]
        mix_count = {n: i + 1 for i, n in enumerate(pieces)}
        copy_count = {n: i + 1 for i, n in enumerate(n for n in leaves if UNITS[n][0][0] == "B")}

        def wait_outputs_left(pe, n):
            if UNITS[n][0][0] == "A":
                pe.wait_ge(mix_ready, mix_count[n])
            else:
                pe.wait_ge(o_copied, copy_count[n])

        def mix_tile(n):
            return UNITS[n][1] + (PAIRS if UNITS[n][0] == "L" else 0)

        def pair(n):
            return 2 + 2 * (order_at[n] % 2)

        def wait_scores_banks(pe, n):
            if order_at[n] < 2:
                return
            former = bank_order[order_at[n] - 2]
            if UNITS[former][0] == "L":
                pe.wait_ge(mix_ready, mix_count[former])
            else:
                pe.wait_ge(exp_done, score_at[former] + 1)

        @block.sync
        def _(sp):
            def load_block(base, i, per, j, src, width, first=False):
                w = base + per * i + j
                slot = (base + j) % RAW_SLOTS
                if not first:
                    sp.wait_ge(split_ready, w - RAW_SLOTS + 1)
                sp.dma_start(raw[slot][:, 0:width], src).then_inc(raw_in[slot], 16)

            sp.dma_start(gains[:], a["gains"]).then_inc(gains_in, 16)
            def first_load(w):
                load_block(w, 0, 0, 0, a["w1gu"][w // 2, :, w % 2, :], KD * P, first=True)

            for i in range(KD // 2):
                sp.dma_start(res[:, 2 * i:2 * i + 2, :], a["x"][:, 2 * i:2 * i + 2, :]).then_inc(x_in[i], 16)
                if i == 0:
                    first_load(0)
            for w in range(1, RAW_SLOTS):
                first_load(w)

            def ffn_loads(base, gu, dn, first):
                with sp.Fori(first, KF // 2) as i:
                    for j in range(4):
                        load_block(base, i, 4, j, a[gu][2 * i + j // 2, :, j % 2, :], KD * P)
                with sp.Fori(0, KD // 2) as i:
                    for j in range(4):
                        load_block(base + 2 * KF, i, 4, j, a[dn][2 * i + j // 2, :, j % 2, :], KF_HALF * P)

            ffn_loads(0, "w1gu", "w1d", 1)
            for c in range(V_BLOCKS):
                load_block(W_V + c, 0, 0, 0, a["w_v"][c], V_K * V_HALF)
            sp.wait_ge(block_used, FFN_BLOCKS)
            sp.dma_start(ident[:], a["ident"]).then_inc(consts_in, 16)
            sp.dma_start(trig[:], a["trig"]).then_inc(consts_in, 16)
            sp.dma_start(small[:], a["small"]).then_inc(consts_in, 16)
            for b in range(len(TILES)):
                load_block(W_TILES + b, 0, 0, 0, a["w_qk"][b], KD * P)
                if b == 0:
                    sp.dma_start(k_all_a[:, 0:A_PAST], a["k_past_a"]).then_inc(cache_in, 16)
                    sp.dma_start(v_past_a[:], a["v_past_a"]).then_inc(cache_in, 16)
                if b == 1:
                    sp.dma_start(k_all_b[:, :, 0:PAST], a["k_past_b"]).then_inc(cache_in, 16)
                    sp.dma_start(v_past_b[:], a["v_past_b"]).then_inc(cache_in, 16)
                if b == 3:
                    sp.wait_ge(rope_done, 1)
                    sp.wait_ge(v_out, 2 * TOK_TILES)
                    sp.dma_start(o["ak_p"], k_a[:, SEQ - A_PAST:SEQ]).then_inc(kv_stored, 16)
                    sp.wait_ge(cache_in, 64)
                    sp.dma_start(o["ak_s"], k_all_a[:, DEC:A_PAST + DEC]).then_inc(kv_stored, 16)
                    sp.dma_start(o["av_p"], v_new[:, SEQ_TILES - 1, 0:P]).then_inc(kv_stored, 16)
                    sp.dma_start(o["av_s"][0:DEC, :], v_past_a[DEC:A_PAST, :]).then_inc(kv_stored, 16)
                    sp.dma_start(o["av_s"][DEC:A_PAST, :], v_new[0:DEC, SEQ_TILES, 0:P]).then_inc(kv_stored, 16)
                    sp.dma_start(o["bv_p"], v_new[:, 0:SEQ_TILES, P:V_COLS]).then_inc(kv_stored, 16)
                    sp.dma_start(o["bv_s"], v_new[0:DEC, SEQ_TILES, P:V_COLS]).then_inc(kv_stored, 16)
                if b >= 8 and b % 2 == 0:
                    h = (b - 8) // 2
                    sp.wait_ge(rope_done, TILES.index(f"kb{h}") + 1)
                    sp.dma_start(o["bk_p"][h], k_b[:, h % 2, :]).then_inc(k_stored[h], 16)
            for i in range(KD):
                load_block(W_OUT + i, 0, 0, 0, a["w_out"][i], KD * P)
                if i == 2:
                    sp.wait_ge(rope_done, len(TILES))
                    h = B_HEADS - 1
                    sp.dma_start(o["bk_p"][h], k_b[:, h % 2, :]).then_inc(k_stored[h], 16)
                    sp.dma_start(o["bk_s"], k_all_b[:, :, PAST:PAST + DEC]).then_inc(kv_stored, 16)
            ffn_loads(W_FFN2, "w2gu", "w2d", 0)
            for t in range(2):
                tok = slice(t * HALF, (t + 1) * HALF)
                sp.wait_ge(y_gp, Y_GP * (t + 1))
                sp.dma_start(o["y"][:, 0:Y_GP, tok], res[:, 0:Y_GP, tok]).then_inc(y_stored, 16)
                for d in range(Y_GP, KD, 2):
                    sp.wait_ge(y_ready, (KD - Y_GP) * t + d - Y_GP + 2)
                    sp.dma_start(o["y"][:, d:d + 2, tok], res[:, d:d + 2, tok]).then_inc(y_stored, 16)
            sp.wait_ge(y_stored, 16 * 2 * (1 + (KD - Y_GP) // 2))
            sp.wait_ge(kv_stored, KV_STORES)
            for h in range(B_HEADS):
                sp.wait_ge(k_stored[h], 16)

        @block.tensor
        def _(pe):
            def block_ready(w):
                pe.wait_ge(split_ready, w + 1)

            def feature_products(bank, slot, k_in_slot, hi, lo, k, first, last, token_halves=(0, 1)):
                col = k_in_slot * P
                for n, (w_part, x_part) in enumerate(((w_hi, hi), (w_hi, lo), (w_lo, hi))):
                    for t in token_halves:
                        m = nc.tensor.matmul(acc[:, bank + t, 0:HALF], w_part[slot][:, col:col + P],
                                             x_part[:, k, t * HALF:(t + 1) * HALF],
                                             start=first and n == 0, stop=last and n == 2)
                return m

            def norm_sums(norm, bank):
                pe.wait_ge(ssq_added, KD * (norm + 1))
                for t in range(2):
                    m = nc.tensor.matmul(acc[:, bank + t, 0:HALF], ones[:], ssq[:, t * HALF:(t + 1) * HALF],
                                         start=True, stop=True)
                m.then_inc(sum_done, 1)

            def gate_up(base, i, ffn, peeled):
                for j in range(2):
                    for part in range(2):
                        q = 2 * j + part
                        block_ready(base + 4 * i + q)
                        bank = 2 * q
                        if not peeled or i > 0:
                            pe.wait_ge((g_out, u_out)[part], KF * ffn + 2 * i + j - 1)
                        elif ffn and j == 0:
                            pe.wait_ge(res_ready, 2 * KD - 1 + part)
                        elif q == 3:
                            pe.wait_ge(rms_done, NORMS_BEFORE[ffn] + 1)
                        for k in range(KD):
                            if peeled and q == 0:
                                pe.wait_ge(u_ready, norms_u(2 * ffn) + k + 1)
                            if peeled and q == 2 and k == 4:
                                norm_sums(2 * ffn, NORM_BANK)
                            m = feature_products(bank, (base + q) % SPLIT_SLOTS, k, u_hi, u_lo, k,
                                                 k == 0, k == KD - 1)
                        m.then_inc(block_used, 1)

            def ffn(base, ffn_no):
                gate_up(base, 0, ffn_no, True)
                with pe.Fori(1, KF // 2) as i:
                    gate_up(base, i, ffn_no, False)
                down = base + 2 * KF

                def down_pair(i, peeled):
                    for j in range(2):
                        if not peeled:
                            pe.wait_ge(res_ready, DOWNS_BEFORE[ffn_no] + 2 * i + j - 1)
                        for c in range(2):
                            q = 2 * j + c
                            block_ready(down + 4 * i + q)
                            for kk in range(KF_HALF):
                                k = c * KF_HALF + kk
                                if peeled and j == 0:
                                    pe.wait_ge(h_ready, KF * ffn_no + k + 1)
                                m = feature_products(2 * j, (down + q) % SPLIT_SLOTS, kk, h_hi, h_lo, k,
                                                     k == 0, k == KF - 1)
                            m.then_inc(block_used, 1)
                pe.wait_ge(u_out, KF * ffn_no + KF - 1)
                down_pair(0, True)
                with pe.Fori(1, KD // 2 - ffn_no) as i:
                    down_pair(i, False)

            def last_down_pair():
                down = BLOCKS - 4
                done = DOWNS_BEFORE[1] + KD - 2
                for q in range(4):
                    if q < 3:
                        block_ready(down + q)
                    if q == 0:
                        pe.wait_ge(res_ready, done - 1)
                    if q < 2:
                        for kk in range(KF_HALF):
                            k = q * KF_HALF + kk
                            m = feature_products(0, (down + q) % SPLIT_SLOTS, kk, h_hi, h_lo, k, k == 0, k == KF - 1)
                        m.then_inc(block_used, 1)
                pe.wait_ge(res_ready, done)
                for t in range(2):
                    for c in range(2):
                        block_ready(down + 2 + c)
                        for kk in range(KF_HALF):
                            k = c * KF_HALF + kk
                            if t == 1 and k == 4:
                                final_sums(0)
                            m = feature_products(2, (down + c) % SPLIT_SLOTS, kk, h_hi, h_lo, k, k == 0, k == KF - 1, (t,))
                    m.then_inc(last_half, 1)
                final_sums(1)

            def final_sums(t):
                bank = FINAL_BANK + t
                tok = slice(t * HALF, (t + 1) * HALF)
                if t == 0:
                    pe.wait_ge(ssq_added, KD * 4 - 1)
                nc.tensor.matmul(acc[:, bank, 0:HALF], ones[:], ssq[:, tok], start=True, stop=False)
                pe.wait_ge(last_sq, t + 1)
                nc.tensor.matmul(acc[:, bank, 0:HALF], ones[:], sq[:, tok], start=False, stop=True).then_inc(sum_done, 1)

            pe.wait_ge(set_up, 2)
            for _ in range(WARM_UP):
                nc.tensor.matmul(acc[:, NORM_BANK, 0:P], ones[:], ones[:], start=True, stop=True)
            ffn(0, 0)

            for c in range(2):
                for kc in range(2):
                    w = W_V + 2 * c + kc
                    block_ready(w)
                    for tt in range(TOK_TILES):
                        n_tok = P if tt < SEQ_TILES else DEC
                        if kc == 0:
                            if c == 1:
                                pe.wait_ge(v_out, tt + 1)
                            elif tt == TOK_TILES - 1:
                                pe.wait_ge(res_ready, KD)
                        for k in range(V_K):
                            kg = V_K * kc + k
                            if c == 0 and tt == 0:
                                pe.wait_ge(u_ready, norms_u(1) + kg + 1)
                            tok = slice(tt * P, tt * P + n_tok)
                            for n, (x_part, w_part) in enumerate(((u_hi, w_hi), (u_hi, w_lo), (u_lo, w_hi))):
                                m = nc.tensor.matmul(
                                    acc[0:n_tok, V_BANK[tt], 0:V_HALF], x_part[:, kg, tok],
                                    w_part[w % SPLIT_SLOTS][:, k * V_HALF:(k + 1) * V_HALF],
                                    start=kg == 0 and n == 0, stop=kg == KD - 1 and n == 2)
                        if kc == 1 and tt < TOK_TILES - 1:
                            m.then_inc(v_done, 1)
                    m.then_inc(block_used, 1)
                    if c == 0 and kc == 0:
                        norm_sums(1, 0)
                        for tt in range(TOK_TILES):
                            n_tok = P if tt < SEQ_TILES else DEC
                            m = nc.tensor.matmul(acc[0:n_tok, TOK_SUM_BANK, tt:tt + 1], ssq[:, tt * P:tt * P + n_tok],
                                                 ones[:, 0:1], start=True, stop=True)
                        m.then_inc(sum_done, 1)

            def scores(n):
                kind, t, i = UNITS[n]
                bank = pair(n)
                names = ("ka", f"qa{t}") if kind[0] == "A" else (f"kb{t}", f"qb{t}")
                pe.wait_ge(rope_done, max(TILES.index(x) for x in names) + 1)
                wait_scores_banks(pe, n)
                if n == 0:
                    pe.wait_ge(v_out, 2 * TOK_TILES)
                if kind in ("As", "Bs"):
                    pe.wait_ge(cache_in, 64)
                if kind == "A":
                    for e in range(2):
                        rows = slice(HEAD * e, HEAD * e + HEAD)
                        for qi in range(2):
                            tile = 2 * i + qi
                            first = max(tile - 1, 0)
                            m = nc.tensor.matmul(
                                acc[:, bank + e, 256 * qi + (P if tile == 0 else 0):256 * (qi + 1)],
                                q_a[rows, t % 2, tile * P:(tile + 1) * P], k_a[rows, first * P:(tile + 1) * P],
                                start=True, stop=True)
                elif kind == "As":
                    m = nc.tensor.matmul(acc[:, bank, 0:A_PAST + DEC], q_diag[:, TILES.index(f"qa{t}") % 2, :],
                                         k_all_a[:], start=True, stop=True)
                elif kind == "B":
                    for e in range(2):
                        rows = slice(HEAD * e, HEAD * e + HEAD)
                        m = nc.tensor.matmul(acc[:, bank + e, 0:(i + 1) * P], q_b[rows, t % 2, i * P:(i + 1) * P],
                                             k_b[rows, t % 2, 0:(i + 1) * P], start=True, stop=True)
                else:
                    for c in range(2):
                        m = nc.tensor.matmul(acc[:, bank + c, 0:HALF], q_diag[:, TILES.index(f"qb{t}") % 2, :],
                                             k_all_b[:, t, c * HALF:(c + 1) * HALF], start=True, stop=True)
                m.then_inc(scores_done, 1)

            def transposes(r):
                n, part = ROUNDS[r]
                kind, t, i = UNITS[n]
                pe.wait_ge(probs_ready, score_at[n] + 1)
                if r == 0:
                    pe.wait_ge(x_out, 2)
                if r:
                    pe.wait_ge(probs_t_ready, r)
                pr = probs[:, score_at[n] % 2, :]
                if kind == "A":
                    for s in range(1 if i == 0 else 0, 4):
                        m = nc.tensor.transpose(acc[:, T_BANK, s * P:(s + 1) * P],
                                                pr[:, BANK * part + s * P:BANK * part + (s + 1) * P], ident[:])
                elif kind == "As":
                    nc.tensor.transpose(acc[:, T_BANK, 0:P], pr[:, 0:P], ident[:])
                    m = nc.tensor.transpose(acc[0:DEC, T_BANK, P:2 * P], pr[:, P:P + DEC], ident[:])
                elif kind == "B":
                    for j in range(i + 1):
                        m = nc.tensor.transpose(acc[:, T_BANK, j * P:(j + 1) * P], pr[:, j * P:(j + 1) * P], ident[:])
                else:
                    for j in range(TOK_TILES):
                        rows = P if j < SEQ_TILES else DEC
                        m = nc.tensor.matmul(acc[0:rows, T_BANK, j * DEC:(j + 1) * DEC],
                                             pr[:, j * P:j * P + rows], diag[:], start=True, stop=True)
                m.then_inc(turned_done, 1)

            def values(r):
                n, part = ROUNDS[r]
                kind, t, i = UNITS[n]
                pe.wait_ge(probs_t_ready, r + 1)
                pt = probs_t[:, r % 2, :]
                if r and leaves_after(*ROUNDS[r - 1]):
                    wait_outputs_left(pe, ROUNDS[r - 1][0])
                if kind == "A":
                    rows = slice(HEAD * part, HEAD * part + HEAD)
                    for qi in range(2):
                        tile = 2 * i + qi
                        for s in range(1 if tile == 0 else 0, 2):
                            m = nc.tensor.matmul(acc[rows, O_BANK, tile * P:(tile + 1) * P],
                                                 v_new[:, tile - 1 + s, HEAD * part:HEAD * part + HEAD],
                                                 pt[:, (2 * qi + s) * P:(2 * qi + s + 1) * P],
                                                 start=s == (tile == 0), stop=s == 1)
                elif kind == "As":
                    for e in range(2):
                        rows = slice(HEAD * e, HEAD * e + HEAD)
                        nc.tensor.matmul(acc[rows, O_BANK, 0:DEC], v_past_a[:, rows], pt[:, e * DEC:(e + 1) * DEC],
                                         start=True, stop=False)
                        m = nc.tensor.matmul(acc[rows, O_BANK, 0:DEC], v_new[0:DEC, SEQ_TILES, rows],
                                             pt[0:DEC, P + e * DEC:P + (e + 1) * DEC], start=False, stop=True)
                elif kind == "B":
                    for j in range(i + 1):
                        m = nc.tensor.matmul(acc[:, O_BANK, i * P:(i + 1) * P], pt[:, j * P:(j + 1) * P],
                                             v_new[:, j, P * (t + 1):P * (t + 2)], start=j == 0, stop=j == i)
                else:
                    for j in range(SEQ_TILES):
                        nc.tensor.matmul(acc[0:DEC, O_BANK, 0:P], pt[:, j * DEC:(j + 1) * DEC],
                                         v_past_b[:, j, P * t:P * (t + 1)], start=j == 0, stop=False)
                    m = nc.tensor.matmul(acc[0:DEC, O_BANK, 0:P], pt[0:DEC, SEQ_TILES * DEC:TOK_TILES * DEC],
                                         v_new[0:DEC, SEQ_TILES, P * (t + 1):P * (t + 2)], start=False, stop=True)
                m.then_inc(o_done, 1)

            def heads_back(n):
                h = UNITS[n][1]
                wait_scores_banks(pe, n)
                pe.wait_ge(ob_ready, h + 1)
                bank = pair(n)
                for tt in range(SEQ_TILES):
                    nc.tensor.transpose(acc[:, bank, tt * P:(tt + 1) * P], o_b[:, h % 2, tt, :], ident[:])
                nc.tensor.transpose(acc[:, bank + 1, 0:DEC], o_b[0:DEC, h % 2, SEQ_TILES, :],
                                    ident[0:DEC, 0:DEC]).then_inc(ob_turned, 1)

            def out_step(d, k):
                bank = 2 * (d % 2)
                if k == 0:
                    block_ready(W_OUT + d)
                    if d >= 2:
                        pe.wait_ge(res_ready, KD + d - 1)
                    elif d == 0:
                        pe.wait_ge(x_out, len(TILES))
                    else:
                        pe.wait_ge(exp_done, len(score_order))
                        pe.wait_ge(mix_ready, mix_count[bank_order[-1]])
                if d == 0:
                    pe.wait_ge(mix_ready, max(c for n, c in mix_count.items() if mix_tile(n) == k))
                m = feature_products(bank, (W_OUT + d) % SPLIT_SLOTS, k, mix_hi, mix_lo, k, k == 0, k == KD - 1)
                if k == KD - 1:
                    m.then_inc(block_used, 1)

            for event in EVENTS:
                if event[0] == "k":
                    _, b, k = event
                    if b == len(TILES):
                        out_step(0, k)
                        continue
                    if k == 0:
                        block_ready(W_TILES + b)
                        if b == 0:
                            pe.wait_ge(rms_done, 2)
                        elif b == 1:
                            pe.wait_ge(v_out, 2 * TOK_TILES - 1)
                        else:
                            pe.wait_ge(x_out, 1 if b == 2 else b)
                    m = feature_products(tile_bank(b), (W_TILES + b) % SPLIT_SLOTS, k, u_hi, u_lo, k, k == 0, k == KD - 1)
                    if k == KD - 1:
                        m.then_inc(block_used, 1)
                elif event[0] == "S":
                    scores(event[1])
                elif event[0] == "T":
                    transposes(event[1])
                elif event[0] == "O":
                    values(event[1])
                elif event[0] == "L":
                    heads_back(event[1])

            for d in range(1, KD):
                for k in range(KD):
                    out_step(d, k)

            ffn(W_FFN2, 1)
            last_down_pair()

        @block.scalar
        def _(act):
            def hi_part(w, width, w_static):
                act.wait_ge(raw_in[w_static % RAW_SLOTS], 16 * arrivals(w, w_static))
                if w_static >= SPLIT_SLOTS:
                    act.wait_ge(block_used, w - SPLIT_SLOTS + 1)
                nc.scalar.activation(w_hi[w_static % SPLIT_SLOTS][:, 0:width],
                                     raw[w_static % RAW_SLOTS][:, 0:width], ACT.Copy).then_inc(hi_ready, 1)

            def arrivals(w, w_static):
                if isinstance(w, int):
                    return w // RAW_SLOTS + 1
                return w_static // RAW_SLOTS + 1 + w.iteration

            class Later:
                def __init__(self, first, i):
                    self.first, self.iteration = first, i

                def __sub__(self, n):
                    return self.first - n + 4 * self.iteration

            def square(d):
                if d >= 2:
                    act.wait_ge(ssq_added, d - 1)
                nc.scalar.activation((sq, up)[d % 2][:], res[:, d, :], ACT.Square).then_inc(sq_ready, 1)

            def rms(count, bank):
                act.wait_ge(sum_done, count + 1)
                nc.scalar.activation(rrow[:, :].rearrange("p (t n) -> p t n", t=2), acc[:, bank:bank + 2, 0:HALF],
                                     ACT.Sqrt, scale=1.0 / D_MODEL, bias=eps[:, 0:1]).then_inc(rms_done, 1)

            def u_hi_part(norm, d):
                nc.scalar.activation(u_hi[:, d, :], res[:, d, :], ACT.Copy,
                                     scale=gains[:, norm, d:d + 1]).then_inc(uhi_ready, 1)

            def static_wait():
                act.wait_ge(gains_in, 16)

            act.wait_ge(gains_in, 16)
            act.wait_ge(set_up, 2)
            nc.scalar.activation(rrow[:, 0:1], eps[:], ACT.Copy)
            for d in range(KD):
                act.wait_ge(x_in[d // 2], 16)
                u_hi_part(0, d)
                if d == 0 or d == KD - 1:
                    w = min(d, 1)
                    hi_part(w, block_width(w), w)
                if d % 2 and d > 1:
                    square(d // 2 - 1)
            square(3)

            def hidden(ffn_no, f):
                act.wait_ge(g_out, KF * ffn_no + f + 1)
                nc.scalar.activation(gate[:], gate[:], ACT.Silu).then_inc(silu_done, 1)
                act.wait_ge(h_full, KF * ffn_no + f + 1)
                nc.scalar.activation(h_hi[:, f, :], up[:], ACT.Copy).then_inc(hhi_ready, 1)

            def first_gate_up(base, ffn_no):
                for w in range(base + 2, base + 6):
                    hi_part(w, block_width(w), w)
                    if w == 2:
                        for d in range(KD // 2, KD):
                            square(d)
                    if w == base + 3:
                        rms(NORMS_BEFORE[ffn_no], NORM_BANK)
                    if w >= base + 4:
                        hidden(ffn_no, w - base - 4)

            def gate_up(base, i, ffn_no):
                for j in range(2):
                    for part in range(2):
                        q = 2 * j + part
                        w_static = base + q + 2
                        w = Later(w_static, i) if not isinstance(i, int) else w_static + 4 * i
                        width = block_width(w) if isinstance(w, int) else KD * P
                        hi_part(w, width, w_static)
                        if part == 0:
                            act.wait_ge(g_out, KF * ffn_no + 2 * i + j + 1)
                            nc.scalar.activation(gate[:], gate[:], ACT.Silu).then_inc(silu_done, 1)
                        else:
                            act.wait_ge(h_full, KF * ffn_no + 2 * i + j + 1)
                            static_wait()
                            nc.scalar.activation(h_hi[:, 2 * i + j, :], up[:], ACT.Copy).then_inc(hhi_ready, 1)

            def residual_next(norm, d, count):
                act.wait_ge(res_ready, count + d + 1)
                act.wait_ge(ssq_added, KD * norm + d)
                static_wait()
                if norm < 3:
                    nc.scalar.activation(u_hi[:, d, :], res[:, d, :], ACT.Copy,
                                         scale=gains[:, norm, bass.ds(d, 1)]).then_inc(uhi_ready, 1)
                nc.scalar.activation(sq[:], res[:, d, :], ACT.Square).then_inc(sq_ready, 1)

            def ffn(base, ffn_no):
                first_gate_up(base, ffn_no)
                with act.Fori(1, KF // 2 - 1) as i:
                    gate_up(base, i, ffn_no)
                gate_up(base, KF // 2 - 1, ffn_no)
                down = base + 2 * KF

                def down_pair(i):
                    for j in range(2):
                        for c in range(2):
                            w_static = down + 2 * j + c + 2
                            w = Later(w_static, i) if not isinstance(i, int) else w_static + 4 * i
                            if not isinstance(w, int) or w < BLOCKS:
                                hi_part(w, block_width(w) if isinstance(w, int) else SLOT, w_static)
                        if ffn_no == 0 or not isinstance(i, int) or j == 0:
                            residual_next(2 * ffn_no + 1, 2 * i + j, DOWNS_BEFORE[ffn_no])
                with act.Fori(0, KD // 2 - 1) as i:
                    down_pair(i)
                down_pair(KD // 2 - 1)

            ffn(0, 0)

            for c in range(2):
                for kc in range(2):
                    w = W_V + 2 * c + kc
                    if kc == 0:
                        hi_part(w + 2, block_width(w + 2), w + 2)
                    if c == 0 and kc == 0:
                        rms(1, 0)
                        act.wait_ge(sum_done, 3)
                        nc.scalar.activation(r_tok[:, 0, 0:SEQ_TILES], acc[:, TOK_SUM_BANK, 0:SEQ_TILES], ACT.Sqrt,
                                             scale=1.0 / D_MODEL, bias=eps[:, 0:1])
                        nc.scalar.activation(r_tok[0:DEC, 0, SEQ_TILES:TOK_TILES],
                                             acc[0:DEC, TOK_SUM_BANK, SEQ_TILES:TOK_TILES], ACT.Sqrt,
                                             scale=1.0 / D_MODEL, bias=eps[0:DEC, 0:1]).then_inc(rms_done, 1)
                    if kc == 1:
                        for tt in range(TOK_TILES):
                            n_tok = P if tt < SEQ_TILES else DEC
                            if tt < TOK_TILES - 1:
                                act.wait_ge(v_done, (TOK_TILES - 1) * c + tt + 1)
                            else:
                                hi_part(w + 2, block_width(w + 2), w + 2)
                                act.wait_ge(block_used, w + 1)
                            act.wait_ge(r_ready, 2)
                            nc.scalar.activation(v_new[0:n_tok, tt, c * V_HALF:(c + 1) * V_HALF],
                                                 acc[0:n_tok, V_BANK[tt], 0:V_HALF], ACT.Copy,
                                                 scale=r_tok[0:n_tok, 1, tt:tt + 1]).then_inc(v_out, 1)

            act.wait_ge(lam_sums, 2)
            nc.scalar.activation(lam[:, 2:4], lam[:, 0:2], ACT.Exp).then_inc(lam_exp, 1)

            def exps(n):
                kind, t, i = UNITS[n]
                sl = score_at[n]
                par = sl % 2
                act.wait_ge(max_ready, sl + 1)
                if sl >= 2:
                    act.wait_ge(turned_done, last_round[score_order[sl - 2]] + 1)
                bank = pair(n)
                pr = probs[:, par, :]
                if kind == "A":
                    nc.scalar.activation(st[:, par, 3, :], st[:, par, 2, :], ACT.Exp)
                    for s in range(4):
                        m = nc.scalar.activation(pr[:, 256 * s:256 * (s + 1)],
                                                 acc[:, bank + s // 2, 256 * (s % 2):256 * (s % 2 + 1)], ACT.Exp,
                                                 scale=SCALE, bias=st[:, par, 1, s:s + 1],
                                                 accum_out=st[:, par, 4, s:s + 1])
                elif kind == "As":
                    nc.scalar.activation(st[:, par, 3, 0:1], st[:, par, 2, 0:1], ACT.Exp)
                    m = nc.scalar.activation(pr[:, 0:A_PAST + DEC], acc[:, bank, 0:A_PAST + DEC], ACT.Exp,
                                             scale=SCALE, bias=st[:, par, 1, 0:1], accum_out=st[:, par, 4, 0:1])
                elif kind == "B":
                    for e in range(2):
                        m = nc.scalar.activation(pr[:, BANK * e:BANK * e + (i + 1) * P], acc[:, bank + e, 0:(i + 1) * P],
                                                 ACT.Exp, scale=SCALE, bias=st[:, par, 1, e:e + 1],
                                                 accum_out=st[:, par, 4, e:e + 1])
                else:
                    m = nc.scalar.activation(pr[:, 0:TOK].rearrange("p (c n) -> p c n", c=2),
                                             acc[:, bank:bank + 2, 0:HALF], ACT.Exp,
                                             scale=SCALE, bias=st[:, par, 1, 0:1], accum_out=st[:, par, 4, 0:1])
                m.then_inc(exp_done, 1)

            def copy_turned(r):
                n, part = ROUNDS[r]
                kind, t, i = UNITS[n]
                act.wait_ge(turned_done, r + 1)
                if r >= 2:
                    act.wait_ge(o_done, r - 1)
                pt = probs_t[:, r % 2, :]
                if kind == "As":
                    nc.scalar.activation(pt[:, 0:P], acc[:, T_BANK, 0:P], ACT.Copy)
                    m = nc.scalar.activation(pt[0:DEC, P:2 * P], acc[0:DEC, T_BANK, P:2 * P], ACT.Copy)
                elif kind == "Bs":
                    nc.scalar.activation(pt[:, 0:4 * DEC], acc[:, T_BANK, 0:4 * DEC], ACT.Copy)
                    m = nc.scalar.activation(pt[0:DEC, 4 * DEC:5 * DEC], acc[0:DEC, T_BANK, 4 * DEC:5 * DEC], ACT.Copy)
                else:
                    cols = slice(P if kind == "A" and i == 0 else 0, BANK if kind == "A" else (i + 1) * P)
                    m = nc.scalar.activation(pt[:, cols], acc[:, T_BANK, cols], ACT.Copy)
                m.then_inc(probs_t_ready, 1)

            def outputs(r):
                n, part = ROUNDS[r]
                kind, t, i = UNITS[n]
                if not leaves_after(n, part):
                    return
                if kind[0] == "B":
                    act.wait_ge(o_copied, copy_count[n])
                    if t:
                        act.wait_ge(ss_ready, t)
                    rows, tt = (slice(0, DEC), slice(SEQ_TILES, TOK_TILES)) if kind == "Bs" else \
                               (slice(0, P), slice(0, SEQ_TILES))
                    nc.scalar.activation(sq_o[rows, tt, :], o_b[rows, t % 2, tt, :],
                                         ACT.Square).then_inc(o_squared, 1)

            def root(n):
                h = UNITS[n][1]
                act.wait_ge(ss_ready, h + 1)
                nc.scalar.activation(ss_o[:, 1, h % 2, 0:TOK_TILES], ss_o[:, 0, h % 2, 0:TOK_TILES], ACT.Sqrt,
                                     scale=1.0 / P, bias=eps[:, 0:1]).then_inc(ss_root, 1)

            def mix_hi_b(n):
                h = UNITS[n][1]
                act.wait_ge(ob_turned, h + 1)
                act.wait_ge(coef_ready, 1)
                bank = pair(n)
                nc.scalar.activation(mix_hi[:, PAIRS + h, 0:SEQ], acc[:, bank, :], ACT.Copy, scale=lam[:, 6:7])
                nc.scalar.activation(mix_hi[:, PAIRS + h, SEQ:TOK], acc[:, bank + 1, 0:DEC], ACT.Copy,
                                     scale=lam[:, 6:7]).then_inc(mixhi_ready, 1)

            for event in EVENTS:
                if event[0] == "k" and event[2] == 1 and event[1] > 0:
                    w = W_TILES + event[1] + 1
                    hi_part(w, block_width(w), w)
                elif event[0] == "S":
                    exps(event[1])
                elif event[0] == "T":
                    copy_turned(event[1])
                elif event[0] == "O":
                    outputs(event[1])
                elif event[0] == "R":
                    root(event[1])
                elif event[0] == "L":
                    mix_hi_b(event[1])

            for d in range(KD):
                w = W_OUT + d
                hi_part(w + 2, block_width(w + 2), w + 2)
                residual_next(2, d, KD)
            ffn(W_FFN2, 1)
            for d in range(Y_GP):
                nc.scalar.activation((gate, up)[d][:], res[:, d, :], ACT.Copy,
                                     scale=gains[:, 3, d:d + 1]).then_inc(y_scaled, 1)
            for t in range(2):
                tok = slice(t * HALF, (t + 1) * HALF)
                act.wait_ge(res_ready, DOWNS_BEFORE[1] + KD + t)
                if t == 0:
                    act.wait_ge(ssq_added, 4 * KD - 1)
                nc.scalar.activation(sq[:, tok], res[:, KD - 1, tok], ACT.Square).then_inc(last_sq, 1)
                act.wait_ge(sum_done, SUMS_BEFORE[3] + 1 + t)
                nc.scalar.activation(rrow[:, tok], acc[:, FINAL_BANK + t, 0:HALF], ACT.Sqrt, scale=1.0 / D_MODEL,
                                     bias=eps[:, 0:1]).then_inc(rms_done, 1)

        @block.vector
        def _(dve):
            chain = [0]

            def then(ins):
                chain[0] += 1
                ins.then_inc(dv, 1)
                dve.wait_ge(dv, chain[0])

            def lo_part(w, width, w_static):
                dve.wait_ge(hi_ready, w + 1)
                nc.vector.tensor_tensor(w_lo[w_static % SPLIT_SLOTS][:, 0:width], raw[w_static % RAW_SLOTS][:, 0:width],
                                        w_hi[w_static % SPLIT_SLOTS][:, 0:width].bitcast(FP32),
                                        ALU.subtract).then_inc(split_ready, 1)

            def u_lo_part(norm, d):
                nc.vector.scalar_tensor_tensor(out=u_lo[:, d, :], in0=res[:, d, :], scalar=gains[:, norm, bass.ds(d, 1)],
                                               in1=u_hi[:, d, :].bitcast(FP32), op0=ALU.mult,
                                               op1=ALU.subtract).then_inc(u_ready, 1)

            nc.vector.memset(ones[:], 1.0).then_inc(set_up, 1)
            nc.vector.memset(eps[:], EPS).then_inc(set_up, 1)
            dve.wait_ge(gains_in, 16)
            for d in range(KD):
                dve.wait_ge(uhi_ready, d + 1)
                u_lo_part(0, d)
                if d == 0 or d == KD - 1:
                    w = min(d, 1)
                    lo_part(w, block_width(w), w)

            def halves(t):
                return t.rearrange("p (t n) -> p t n", t=2)

            def gate_out(base, blocks, j):
                dve.wait_ge(block_used, base + blocks + 1)
                nc.vector.tensor_tensor(halves(gate[:, :]), acc[:, 4 * j:4 * j + 2, 0:HALF], halves(rrow[:, :]),
                                        ALU.mult).then_inc(g_out, 1)

            def up_out(base, blocks, j):
                dve.wait_ge(block_used, base + blocks + 2)
                nc.vector.tensor_tensor(halves(up[:, :]), acc[:, 4 * j + 2:4 * j + 4, 0:HALF], halves(rrow[:, :]),
                                        ALU.mult).then_inc(u_out, 1)

            def hidden(ffn_no, f):
                dve.wait_ge(u_out, KF * ffn_no + f + 1)
                dve.wait_ge(silu_done, KF * ffn_no + f + 1)
                nc.vector.tensor_tensor(up[:], up[:], gate[:], ALU.mult).then_inc(h_full, 1)
                dve.wait_ge(h_full, KF * ffn_no + f + 1)
                dve.wait_ge(hhi_ready, KF * ffn_no + f + 1)
                nc.vector.tensor_tensor(h_lo[:, f, :], up[:], h_hi[:, f, :].bitcast(FP32),
                                        ALU.subtract).then_inc(h_ready, 1)

            def first_gate_up(base, ffn_no):
                for w in (base + 2, base + 3):
                    lo_part(w, block_width(w), w)
                dve.wait_ge(rms_done, NORMS_BEFORE[ffn_no] + 1)
                nc.vector.reciprocal(rrow[:], rrow[:]).then_inc(r_ready, 1)
                dve.wait_ge(r_ready, NORMS_BEFORE[ffn_no] + 1)
                for f in range(2):
                    if f == 1:
                        lo_part(base + 5, block_width(base + 5), base + 5)
                    gate_out(base, 2 * f, f)
                    if f == 1:
                        dve.wait_ge(h_ready, KF * ffn_no + 1)
                    up_out(base, 2 * f, f)
                    if f == 0:
                        lo_part(base + 4, block_width(base + 4), base + 4)
                    hidden(ffn_no, f)

            def gate_up(base, i, ffn_no):
                for j in range(2):
                    f = 2 * i + j
                    w = base + 4 * i + 2 * j + 2
                    w_static = base + 2 * j + 2
                    lo_part(w, block_width(w) if isinstance(w, int) else KD * P, w_static)
                    gate_out(base, 4 * i + 2 * j, j)
                    lo_part(w + 1, block_width(w + 1) if isinstance(w, int) else KD * P, w_static + 1)
                    up_out(base, 4 * i + 2 * j, j)
                    hidden(ffn_no, f)

            def next_u(norm, d):
                dve.wait_ge(uhi_ready, norms_u(norm) + d + 1)
                u_lo_part(norm, d)

            def ffn(base, ffn_no):
                first_gate_up(base, ffn_no)
                with dve.Fori(1, KF // 2 - 1) as i:
                    gate_up(base, i, ffn_no)
                gate_up(base, KF // 2 - 1, ffn_no)
                down = base + 2 * KF

                def down_pair(i):
                    for j in range(2):
                        d = 2 * i + j
                        for c in range(2):
                            w = down + 4 * i + 2 * j + c + 2
                            if not isinstance(w, int) or w < BLOCKS:
                                lo_part(w, block_width(w) if isinstance(w, int) else SLOT, down + 2 * j + c + 2)
                        if ffn_no and isinstance(i, int) and j == 1:
                            break
                        dve.wait_ge(block_used, down + 4 * i + 2 * j + 2)
                        nc.vector.scalar_tensor_tensor(out=halves(res[:, d, :]), in0=acc[:, 2 * j:2 * j + 2, 0:HALF],
                                                       scalar=0.5, in1=halves(res[:, d, :]), op0=ALU.mult,
                                                       op1=ALU.add).then_inc(res_ready, 1)
                        if ffn_no == 0:
                            next_u(1, d)
                with dve.Fori(0, KD // 2 - 1) as i:
                    down_pair(i)
                down_pair(KD // 2 - 1)

            ffn(0, 0)

            for c in range(2):
                for kc in range(2):
                    w = W_V + 2 * c + kc
                    lo_part(w + 2, block_width(w + 2), w + 2)
                    if c == 0 and kc == 0:
                        dve.wait_ge(rms_done, 3)
                        nc.vector.reciprocal(r_tok[:, 1, 0:SEQ_TILES], r_tok[:, 0, 0:SEQ_TILES])
                        nc.vector.reciprocal(r_tok[0:DEC, 1, SEQ_TILES:TOK_TILES],
                                             r_tok[0:DEC, 0, SEQ_TILES:TOK_TILES]).then_inc(r_ready, 1)
                        nc.vector.reciprocal(rrow[:], rrow[:]).then_inc(r_ready, 1)
            dve.wait_ge(consts_in, 48)
            for e in range(2):
                nc.vector.tensor_tensor_reduce(out=sq_o[:, e, 0:HEAD], in0=lvec[:, 2 * e, :],
                                               in1=lvec[:, 2 * e + 1, :], scale=1.0, scalar=0.0,
                                               op0=ALU.mult, op1=ALU.add,
                                               accum_out=lam[:, e:e + 1]).then_inc(lam_sums, 1)
            then(nc.vector.tensor_tensor(ident2[:], ident[:, 0:DEC], ident[:, DEC:2 * DEC], ALU.add))
            dve.wait_ge(lam_sums, 2)
            nc.vector.memset(sq_o[:], 1.0)
            then(nc.vector.memset(o_b[:], 0.0))
            dve.wait_ge(lam_exp, 1)
            then(nc.vector.tensor_tensor(lam[:, 4:5], lam[:, 3:4], lam[:, 2:3], ALU.subtract))
            then(nc.vector.tensor_scalar(lam[:, 4:5], lam[:, 4:5], -LAM_INIT, None, ALU.add))
            nc.vector.memset(lam[0:HEAD, 5:6], 1.0)
            nc.vector.tensor_copy(lam[HEAD:P, 5:6], lam[HEAD:P, 4:5])
            then(nc.vector.tensor_scalar(lam[:, 6:7], gsub, 1.0 - LAM_INIT, None, ALU.mult))
            nc.vector.tensor_copy(lam[:, 7:8], lam[:, 6:7]).then_inc(coef_ready, 1)

            def take_projection(b):
                dve.wait_ge(block_used, W_TILES + b + 1)
                if b == 0:
                    dve.wait_ge(trig_ready, 2)
                else:
                    dve.wait_ge(rope_done, b)
                src = acc[:, tile_bank(b):tile_bank(b) + 2, 0:HALF]
                nc.vector.stream_shuffle(halves(turned[:, :]), src,
                                         [(i + 16) % 32 for i in range(32)]).then_inc(turn_done, 1)
                nc.vector.tensor_tensor(halves(rope_x[:, :]), src, halves(trig_r[:, 0, :]),
                                        ALU.mult).then_inc(x_out, 1)

            def maxima(n):
                kind, t, i = UNITS[n]
                sl = score_at[n]
                par = sl % 2
                bank = pair(n)
                s = st[:, par]
                dve.wait_ge(scores_done, sl + 1)
                if kind == "A":
                    v = acc[:, bank:bank + 2, :].rearrange("p b (q n) -> p (b q) n", q=2)
                    nc.vector.memset(v[0:CHUNK, :, 192:256], NEG)
                    if i == 0:
                        nc.vector.memset(acc[:, bank:bank + 2, 0:P], NEG)
                        then(nc.vector.memset(acc[CHUNK:P, bank:bank + 2, 256:256 + CHUNK], NEG))
                    else:
                        then(nc.vector.memset(v[CHUNK:P, :, 0:CHUNK], NEG))
                    then(nc.vector.reduce_max(s[:, 0, 0:4], v, AX.X))
                    cols, sink = slice(0, 4), sink_p[:, t, :]
                elif kind == "As":
                    then(nc.vector.reduce_max(s[:, 0, 0:1], acc[:, bank, 0:A_PAST + DEC], AX.X))
                    cols, sink = slice(0, 1), sink_s[:, t:t + 1]
                elif kind == "B":
                    then(nc.vector.memset(acc[0:CHUNK, bank:bank + 2, i * P + CHUNK:(i + 1) * P], NEG))
                    then(nc.vector.reduce_max(s[:, 0, 0:2], acc[:, bank:bank + 2, 0:(i + 1) * P], AX.X))
                else:
                    then(nc.vector.reduce_max(s[:, 0, 0:1], acc[:, bank:bank + 2, 0:HALF], AX.XY))
                if kind[0] == "A":
                    then(nc.vector.scalar_tensor_tensor(out=s[:, 0, cols], in0=s[:, 0, cols], scalar=SCALE, in1=sink,
                                                        op0=ALU.mult, op1=ALU.max))
                    nc.vector.tensor_scalar(s[:, 1, cols], s[:, 0, cols], -1.0, None, ALU.mult)
                    nc.vector.tensor_tensor(s[:, 2, cols], sink, s[:, 0, cols], ALU.subtract).then_inc(max_ready, 1)
                else:
                    cols = slice(0, 2 if kind == "B" else 1)
                    nc.vector.tensor_scalar(s[:, 1, cols], s[:, 0, cols], -SCALE, None, ALU.mult).then_inc(max_ready, 1)

            def normalise(n):
                kind, t, i = UNITS[n]
                sl = score_at[n]
                par = sl % 2
                s = st[:, par]
                pr = probs[:, par, :]
                dve.wait_ge(exp_done, sl + 1)
                cols = slice(0, {"A": 4, "As": 1, "B": 2, "Bs": 1}[kind])
                if kind[0] == "A":
                    then(nc.vector.tensor_tensor(s[:, 4, cols], s[:, 4, cols], s[:, 3, cols], ALU.add))
                then(nc.vector.reciprocal(s[:, 5, cols], s[:, 4, cols]))
                if kind == "A":
                    for q in range(4):
                        m = nc.vector.tensor_scalar(pr[:, 256 * q:256 * (q + 1)], pr[:, 256 * q:256 * (q + 1)],
                                                    s[:, 5, q:q + 1], None, ALU.mult)
                elif kind == "As":
                    m = nc.vector.tensor_scalar(pr[:, 0:A_PAST + DEC], pr[:, 0:A_PAST + DEC], s[:, 5, 0:1], None, ALU.mult)
                elif kind == "B":
                    nc.vector.tensor_tensor(s[:, 6, 0:1], s[:, 5, 1:2], lam[:, 4:5], ALU.mult)
                    w = (i + 1) * P
                    then(nc.vector.tensor_scalar(pr[:, 0:w], pr[:, 0:w], s[:, 5, 0:1], None, ALU.mult))
                    m = nc.vector.scalar_tensor_tensor(out=pr[:, 0:w], in0=pr[:, BANK:BANK + w], scalar=s[:, 6, 0:1],
                                                       in1=pr[:, 0:w], op0=ALU.mult, op1=ALU.add)
                else:
                    then(nc.vector.tensor_tensor(s[:, 6, 0:1], s[:, 5, 0:1], lam[:, 5:6], ALU.mult))
                    if t:
                        dve.wait_ge(turned_done, last_round[units_bs[t - 1]] + 1)
                    m = nc.vector.tensor_scalar(diag[:], ident2[:], s[:, 6, 0:1], None, ALU.mult)
                m.then_inc(probs_ready, 1)

            def outputs(r):
                n, part = ROUNDS[r]
                kind, t, i = UNITS[n]
                if not leaves_after(n, part):
                    return
                dve.wait_ge(o_done, r + 1)
                sample = kind[1:] == "s"
                if kind[0] == "A":
                    to = slice(SEQ, TOK) if sample else slice(0, SEQ)
                    src = acc[:, O_BANK, 0:DEC] if sample else acc[:, O_BANK, :]
                    then(nc.vector.tensor_copy(mix_hi[:, t, to], src))
                    nc.vector.tensor_tensor(mix_lo[:, t, to], src, mix_hi[:, t, to].bitcast(FP32),
                                            ALU.subtract).then_inc(mix_ready, 1)
                elif sample:
                    if t >= 2:
                        dve.wait_ge(ob_turned, t - 1)
                    nc.vector.tensor_copy(o_b[0:DEC, t % 2, SEQ_TILES, :], acc[0:DEC, O_BANK, 0:P]).then_inc(o_copied, 1)
                else:
                    nc.vector.tensor_copy(o_b[:, t % 2, 0:SEQ_TILES, :],
                                          acc[:, O_BANK, :].rearrange("p (t n) -> p t n", t=SEQ_TILES)).then_inc(o_copied, 1)

            def head_squares(n):
                t = UNITS[n][1]
                dve.wait_ge(o_squared, 2 * t + 2)
                nc.vector.tensor_reduce(ss_o[:, 0, t % 2, 0:TOK_TILES], sq_o[:], AX.X,
                                        ALU.add).then_inc(ss_ready, 1)

            def head_norm(n):
                h = UNITS[n][1]
                head_squares(n)
                dve.wait_ge(ss_root, h + 1)
                then(nc.vector.reciprocal(ss_o[:, 2, h % 2, 0:TOK_TILES], ss_o[:, 1, h % 2, 0:TOK_TILES]))
                for tt in range(TOK_TILES):
                    m = nc.vector.tensor_scalar(o_b[:, h % 2, tt, :], o_b[:, h % 2, tt, :],
                                                ss_o[:, 2, h % 2, tt:tt + 1], None, ALU.mult)
                m.then_inc(ob_ready, 1)

            def heads_back(n):
                h = UNITS[n][1]
                bank = pair(n)
                dve.wait_ge(mixhi_ready, h + 1)
                nc.vector.scalar_tensor_tensor(out=mix_lo[:, PAIRS + h, 0:SEQ], in0=acc[:, bank, :], scalar=lam[:, 6:7],
                                               in1=mix_hi[:, PAIRS + h, 0:SEQ].bitcast(FP32), op0=ALU.mult,
                                               op1=ALU.subtract)
                nc.vector.scalar_tensor_tensor(out=mix_lo[:, PAIRS + h, SEQ:TOK], in0=acc[:, bank + 1, 0:DEC],
                                               scalar=lam[:, 6:7], in1=mix_hi[:, PAIRS + h, SEQ:TOK].bitcast(FP32),
                                               op0=ALU.mult, op1=ALU.subtract).then_inc(mix_ready, 1)

            for event in EVENTS:
                if event[0] == "k" and event[2] == KD - 1 and event[1] < len(TILES):
                    take_projection(event[1])
                elif event[0] == "k" and event[2] == 1 and event[1] > 0:
                    w = W_TILES + event[1] + 1
                    lo_part(w, block_width(w), w)
                elif event[0] == "S":
                    maxima(event[1])
                elif event[0] == "N":
                    normalise(event[1])
                elif event[0] == "O":
                    outputs(event[1])
                elif event[0] == "R":
                    head_norm(event[1])
                elif event[0] == "L":
                    heads_back(event[1])

            for d in range(KD):
                w = W_OUT + d
                lo_part(w + 2, block_width(w + 2), w + 2)
                dve.wait_ge(block_used, w + 1)
                bank = 2 * (d % 2)
                nc.vector.tensor_tensor(halves(res[:, d, :]), acc[:, bank:bank + 2, 0:HALF], halves(res[:, d, :]),
                                        ALU.add).then_inc(res_ready, 1)
                next_u(2, d)
            dve.wait_ge(kv_stored, KV_STORES)
            for h in range(B_HEADS):
                dve.wait_ge(k_stored[h], 16)
            ffn(W_FFN2, 1)

            for t in range(2):
                tok = slice(t * HALF, (t + 1) * HALF)
                dve.wait_ge(last_half, t + 1)
                nc.vector.scalar_tensor_tensor(out=res[:, KD - 1, tok], in0=acc[:, 2 + t, 0:HALF], scalar=0.5,
                                               in1=res[:, KD - 1, tok], op0=ALU.mult, op1=ALU.add).then_inc(res_ready, 1)
                dve.wait_ge(rms_done, NORMS_BEFORE[1] + 2 + t)
                nc.vector.reciprocal(rrow[:, tok], rrow[:, tok]).then_inc(final_r, 1)
                dve.wait_ge(final_r, t + 1)
                dve.wait_ge(res_ready, DOWNS_BEFORE[1] + KD + t)
                for d in range(Y_GP, KD):
                    nc.vector.scalar_tensor_tensor(out=res[:, d, tok], in0=res[:, d, tok],
                                                   scalar=gains[:, 3, d:d + 1], in1=rrow[:, tok], op0=ALU.mult,
                                                   op1=ALU.mult).then_inc(y_ready, 1)

        @block.gpsimd
        def _(gp):
            steps = [0]

            def then(ins):
                steps[0] += 1
                ins.then_inc(gp_step, 1)
                gp.wait_ge(gp_step, steps[0])

            def clear_sums(norm):
                nc.gpsimd.memset(ssq[:], 0.0).then_inc(ssq_zero, 1)
                gp.wait_ge(ssq_zero, norm + 1)

            def sums(norm):
                gp.wait_ge(sum_done, SUMS_BEFORE[norm])
                clear_sums(norm)
                with gp.Fori(0, KD - 1 if norm == 3 else KD) as d:
                    gp.wait_ge(sq_ready, KD * norm + d + 1)
                    gp.wait_ge(ssq_added, KD * norm + d)
                    nc.gpsimd.tensor_tensor(ssq[:], ssq[:], sq[:], ALU.add).then_inc(ssq_added, 1)

            clear_sums(0)
            with gp.Fori(0, KD // 2) as i:
                for j in range(2):
                    gp.wait_ge(sq_ready, 2 * i + j + 1)
                    gp.wait_ge(ssq_added, 2 * i + j)
                    nc.gpsimd.tensor_tensor(ssq[:], ssq[:], (sq, up)[j][:], ALU.add).then_inc(ssq_added, 1)
            sums(1)
            gp.wait_ge(block_used, FFN_BLOCKS)
            nc.gpsimd.memset(q_diag[:], 0.0).then_inc(zeroed, 1)
            gp.wait_ge(r_ready, 3)
            gp.wait_ge(consts_in, 48)
            for c in range(2):
                nc.gpsimd.tensor_tensor(trig_r[:, c, :], trig[:, c, :], rrow[:], ALU.mult).then_inc(trig_ready, 1)
            gp.wait_ge(trig_ready, 2)
            gp.wait_ge(zeroed, 1)

            for b, name in enumerate(TILES):
                gp.wait_ge(turn_done, b + 1)
                then(nc.gpsimd.tensor_tensor(turned[:], turned[:], trig_r[:, 1, :], ALU.mult))
                gp.wait_ge(x_out, b + 1)
                if name == "ka":
                    nc.gpsimd.tensor_tensor(k_a[:], rope_x[:, 0:SEQ], turned[:, 0:SEQ], ALU.add)
                    m = nc.gpsimd.tensor_tensor(k_all_a[:, A_PAST:A_PAST + DEC], rope_x[:, SEQ:TOK],
                                                turned[:, SEQ:TOK], ALU.add)
                else:
                    slot = int(name[2]) % 2
                    former = [n for c in range(b) if TILES[c][0:2] == name[0:2] and int(TILES[c][2]) % 2 == slot
                              for n in tile_users(c)]
                    if former:
                        gp.wait_ge(scores_done, max(score_at[n] for n in former) + 1)
                    if name[0] == "k":
                        if int(name[2]) >= 2:
                            gp.wait_ge(k_stored[int(name[2]) - 2], 16)
                        nc.gpsimd.tensor_tensor(k_b[:, slot, :], rope_x[:, 0:SEQ], turned[:, 0:SEQ], ALU.add)
                        m = nc.gpsimd.tensor_tensor(k_all_b[:, int(name[2]), PAST:PAST + DEC], rope_x[:, SEQ:TOK],
                                                    turned[:, SEQ:TOK], ALU.add)
                    else:
                        dst = q_a if name[1] == "a" else q_b
                        then(nc.gpsimd.tensor_tensor(dst[:, slot, :], rope_x[:, 0:SEQ], turned[:, 0:SEQ], ALU.add))
                        before = [n for c in range(b) if TILES[c][0] == "q" and c % 2 == b % 2
                                  for n in tile_users(c) if UNITS[n][0][1:] == "s"]
                        if before:
                            gp.wait_ge(scores_done, max(score_at[n] for n in before) + 1)
                        for e in range(2):
                            rows = slice(HEAD * e, HEAD * e + HEAD)
                            m = nc.gpsimd.tensor_tensor(q_diag[rows, b % 2, rows], rope_x[rows, SEQ:TOK],
                                                        turned[rows, SEQ:TOK], ALU.add)
                            if e == 0:
                                then(m)
                m.then_inc(rope_done, 1)
                gp.wait_ge(rope_done, b + 1)
            sums(2)
            sums(3)
            gp.wait_ge(y_scaled, Y_GP)
            for part in range(2):
                gp.wait_ge(final_r, part + 1)
                tok = slice(part * HALF, (part + 1) * HALF)
                for d in range(Y_GP):
                    nc.gpsimd.tensor_tensor(res[:, d, tok], (gate, up)[d][:, tok], rrow[:, tok],
                                            ALU.mult).then_inc(y_gp, 1)


KV_STORES = 16 * 8
NORMS_BEFORE = (0, 3)
SUMS_BEFORE = (0, 1, 3, 4)
DOWNS_BEFORE = (0, 2 * KD)
last_round = {u: r for r, (u, _) in enumerate(ROUNDS)}
units_bs = [n for n, u in enumerate(UNITS) if u[0] == "Bs"]

HEAD_ORDER = np.concatenate([np.arange(0, 16), np.arange(32, 48), np.arange(16, 32), np.arange(48, 64)])


def kernel(**inputs):
    import concourse.bacc as bacc
    from concourse.bass_utils import run_bass_kernel_spmd

    x = {k: np.ascontiguousarray(v) for k, v in inputs.items()}
    f32 = np.float32

    def tiled(w, cols):
        k, n = w.shape
        return w.reshape(k // P, P, n // cols, cols).transpose(2, 1, 0, 3).reshape(n // cols, P, -1)

    def gate_up(g, u):
        return np.stack([tiled(g, P), tiled(u, P)], axis=2)

    def down(w):
        t = tiled(w, P).reshape(KD, P, 2, -1)
        return t

    def per_partition(v):
        return v.reshape(-1, P).T

    xt = np.concatenate([x["x_prompt"][0], x["x_sample"][0]], axis=0)
    xt = xt.T.reshape(KD, P, TOK).transpose(1, 0, 2)

    w_in = x["w_in"][0]
    cuts = np.cumsum([512, 128, 128, 512, 512])
    wqa, wka, wva, wqb, wkb, wvb = np.split(w_in, cuts, axis=1)

    def head_cols(w, heads):
        return np.concatenate([w[:, h * HEAD + HEAD_ORDER] for h in heads], axis=1)

    groups = [head_cols(wka, (0, 1))] + [head_cols(wqa, (t, t + PAIRS)) for t in range(PAIRS)]
    for h in range(B_HEADS):
        groups += [head_cols(wkb, (2 * h, 2 * h + 1)), head_cols(wqb, (2 * h, 2 * h + 1))]
    w_qk = np.concatenate([tiled(g, P) for g in groups], axis=0)
    w_v = np.concatenate([wva, wvb], axis=1)
    w_v = np.stack([tiled(w_v[512 * kc:512 * (kc + 1)], V_HALF)[c] for c in range(2) for kc in range(2)])
    rows = np.concatenate([np.r_[t * HEAD:(t + 1) * HEAD, (t + PAIRS) * HEAD:(t + PAIRS + 1) * HEAD]
                           for t in range(PAIRS)] + [np.arange(512, 1024)])
    w_out = tiled(x["w_out"][0][rows], P)

    def keys(c, heads):
        c = c[:, :, HEAD_ORDER]
        return c.transpose(1, 2, 0).reshape(heads // 2, P, -1)

    pos = np.arange(TOK).astype(f32)
    inv = (10000.0 ** (-np.arange(32) / 32.0)).astype(f32)
    ang = (pos[None, :] * inv[:, None]).astype(np.float64)
    dims = np.tile(HEAD_ORDER, 2)
    trig = np.stack([np.cos(ang)[dims % 32], np.sin(ang)[dims % 32] * np.where(dims < 32, -1.0, 1.0)[:, None]],
                    axis=1).astype(f32)
    sinks = x["attn_sinks"][0]
    sink_p = np.stack([sinks[[t, t, t + PAIRS, t + PAIRS]] for t in range(PAIRS)]).reshape(1, 16)
    sink_s = np.concatenate([np.tile(sinks[0:4], (HEAD, 1)), np.tile(sinks[4:8], (HEAD, 1))], axis=0)
    lam = np.concatenate([x[n][0] for n in ("lambda_q1", "lambda_k1", "lambda_q2", "lambda_k2")])[None]
    small = np.concatenate([np.tile(sink_p, (P, 1)), sink_s, x["subln_norm"][0][:, None], np.tile(lam, (P, 1))], axis=1)
    gains = np.stack([per_partition(x[n].reshape(-1)) for n in ("ffn1_norm", "mix_norm", "ffn2_norm", "final_norm")],
                     axis=1)
    arrays = {
        "gains": gains, "x": xt,
        "w1gu": gate_up(x["ffn1_w_gate"][0], x["ffn1_w_up"][0]), "w1d": down(x["ffn1_w_down"][0]),
        "w2gu": gate_up(x["ffn2_w_gate"][0], x["ffn2_w_up"][0]), "w2d": down(x["ffn2_w_down"][0]),
        "w_v": w_v, "w_qk": w_qk, "w_out": w_out,
        "ident": np.eye(P, dtype=f32), "trig": trig, "small": small,
        "k_past_a": keys(x["cache_a_k"][0, 0], 2)[0], "v_past_a": x["cache_a_v"][0, 0].reshape(A_PAST, P),
        "k_past_b": keys(x["cache_b_k"][0, 0], 8).transpose(1, 0, 2),
        "v_past_b": x["cache_b_v"][0, 0].reshape(SEQ_TILES, P, 512).transpose(1, 0, 2),
    }
    arrays = {k: np.ascontiguousarray(v) for k, v in arrays.items()}
    outs = {
        "y": (P, KD, TOK), "ak_p": (P, A_PAST), "av_p": (A_PAST, P), "bk_p": (B_HEADS, P, SEQ),
        "bv_p": (P, SEQ_TILES, 512), "ak_s": (P, A_PAST), "av_s": (A_PAST, P), "bk_s": (P, B_HEADS, DEC),
        "bv_s": (DEC, 512),
    }
    nc = bacc.Bacc("TRN2", target_bir_lowering=False, num_devices=1, dynamic_dma_scratch_size=1024)
    a = {k: nc.dram_tensor(f"in_{k}", v.shape, mybir.dt.from_np(v.dtype), kind="ExternalInput").ap()
         for k, v in arrays.items()}
    o = {k: nc.dram_tensor(f"out_{k}", s, FP32, kind="ExternalOutput").ap() for k, s in outs.items()}
    hybrid_step(nc, a, o)
    r = run_bass_kernel_spmd(nc, [{f"in_{k}": v for k, v in arrays.items()}], core_ids=[0])
    g = {k: np.asarray(r.results[0][f"out_{k}"]) for k in outs}

    back = np.argsort(HEAD_ORDER)

    def keys_back(k, heads):
        return k.reshape(heads, HEAD, -1)[:, back].transpose(2, 0, 1)

    y = g["y"].transpose(1, 0, 2).reshape(D_MODEL, TOK).T
    return (
        y[None, :SEQ], y[None, SEQ:],
        keys_back(g["ak_p"], 2)[None, None], g["av_p"].reshape(1, 1, A_PAST, 2, HEAD),
        keys_back(g["bk_p"], 8)[None, None],
        g["bv_p"].transpose(1, 0, 2).reshape(1, 1, SEQ, B_HEADS, P),
        keys_back(g["ak_s"], 2)[None, None], g["av_s"].reshape(1, 1, A_PAST, 2, HEAD),
        keys_back(g["bk_s"].transpose(1, 0, 2), 8)[None, None], g["bv_s"].reshape(1, 1, DEC, B_HEADS, P),
    )
```
